# Optimizing a Trainium2 kernel written in Bass

```python
import math
import jax, jax.numpy as jnp
from jax import lax
import numpy as np

D_MODEL = 2048
BATCH = 1
SEQ = 256
DEPTH = 1

POOL_WIDTH = D_MODEL // 2
POOL_WINDOWS = (2, 4, 8, 16)
POOL_GROUPS = len(POOL_WINDOWS)
POOL_GROUP_DIM = POOL_WIDTH // POOL_GROUPS
SB_HEAD_DIM = 128
SB_HEADS = (D_MODEL // 2) // SB_HEAD_DIM
SB_WIDTH = SB_HEADS * SB_HEAD_DIM
N_BRANCHES = 2
IN_WIDTH = POOL_WIDTH + 3 * SB_WIDTH + N_BRANCHES * D_MODEL
D_FF = 4 * D_MODEL
Q_BLOCK = 128
N_MOD = 6
EPS = 1e-6


def rms_norm(x, w):
    xf = x.astype(jnp.float32)
    y = xf * lax.rsqrt(jnp.mean(jnp.square(xf), axis=-1, keepdims=True) + EPS)
    return (y * w.astype(jnp.float32)).astype(x.dtype)

def multiscale_pool(u, w_pool, pool_scale):
    B, S, _ = u.shape
    uf = u.astype(jnp.float32).reshape(B, S, POOL_GROUPS, POOL_GROUP_DIM)
    cs = jnp.cumsum(uf, axis=1)
    pos = jnp.arange(S, dtype=jnp.int32)
    outs = []
    for g, w in enumerate(POOL_WINDOWS):
        csg = cs[:, :, g]
        lag = jnp.pad(csg, ((0, 0), (w, 0), (0, 0)))[:, :S]
        count = jnp.minimum(pos + 1, w).astype(jnp.float32)[None, :, None]
        outs.append((csg - lag) / count - uf[:, :, g])
    pooled = jnp.stack(outs, axis=2)
    mixed = jnp.einsum('bsgc,gce->bsge', pooled, w_pool.astype(jnp.float32))
    y = mixed.reshape(B, S, POOL_WIDTH) * pool_scale.astype(jnp.float32)
    return y.astype(u.dtype)

def stick_breaking_attention(q, k, v):
    B, S, H, Dh = q.shape
    nb = S // Q_BLOCK
    scale = 1.0 / math.sqrt(Dh)
    kh = k.transpose(0, 2, 1, 3)
    vh = v.transpose(0, 2, 1, 3)
    qb = q.transpose(0, 2, 1, 3).reshape(B, H, nb, Q_BLOCK, Dh).transpose(2, 0, 1, 3, 4)
    starts = jnp.arange(nb, dtype=jnp.int32) * Q_BLOCK
    key_pos = jnp.arange(S, dtype=jnp.int32)

    def block(args):
        q_blk, t0 = args
        z = jnp.einsum('bhqd,bhkd->bhqk', q_blk, kh).astype(jnp.float32) * scale
        q_pos = t0 + jnp.arange(Q_BLOCK, dtype=jnp.int32)
        mask = key_pos[None, :] < q_pos[:, None]
        log_beta = jax.nn.log_sigmoid(z)
        log_1m_beta = log_beta - z
        l = jnp.where(mask, log_1m_beta, 0.0)
        suffix = lax.cumsum(l, axis=3, reverse=True) - l
        a = jnp.where(mask, jnp.exp(log_beta + suffix), 0.0)
        return jnp.einsum('bhqk,bhkd->bhqd', a.astype(vh.dtype), vh)

    out = lax.map(block, (qb, starts))
    return out.transpose(1, 0, 3, 2, 4).reshape(B, S, H * Dh)

def first_inputs(seed: int = 0) -> dict:
    key = jax.random.key(seed)
    ks = jax.random.split(key, 20)
    f32 = jnp.float32
    L = DEPTH

    def nrm(k, shape, fan_in, gain=1.0):
        return jax.random.normal(k, shape, f32) * (gain * fan_in ** -0.5)

    return {
        "x": jax.random.normal(ks[0], (BATCH, SEQ, D_MODEL), f32),
        "c": jax.random.normal(ks[1], (BATCH, D_MODEL), f32),
        "w_ada": nrm(ks[2], (L, D_MODEL, N_MOD * D_MODEL), D_MODEL, 0.5),
        "b_ada": 0.02 * jax.random.normal(ks[3], (L, N_MOD * D_MODEL), f32),
        "norm1_w": 1.0 + 0.05 * jax.random.normal(ks[4], (L, D_MODEL), f32),
        "w_in": nrm(ks[5], (L, D_MODEL, IN_WIDTH), D_MODEL),
        "q_norm_w": 1.0 + 0.05 * jax.random.normal(ks[6], (L, SB_HEAD_DIM), f32),
        "k_norm_w": 1.0 + 0.05 * jax.random.normal(ks[7], (L, SB_HEAD_DIM), f32),
        "w_pool": nrm(ks[8], (L, POOL_GROUPS, POOL_GROUP_DIM, POOL_GROUP_DIM), POOL_GROUP_DIM),
        "pool_scale": 1.0 + 0.1 * jax.random.normal(ks[9], (L, POOL_WIDTH), f32),
        "w_a_up": nrm(ks[10], (L, POOL_WIDTH, D_MODEL), POOL_WIDTH),
        "w_b_up": nrm(ks[11], (L, SB_WIDTH, D_MODEL), SB_WIDTH),
        "w_o": nrm(ks[12], (L, D_MODEL, D_MODEL), D_MODEL),
        "norm2_w": 1.0 + 0.05 * jax.random.normal(ks[13], (L, D_MODEL), f32),
        "w_ff1": nrm(ks[14], (L, D_MODEL, D_FF), D_MODEL),
        "w_ff2": nrm(ks[15], (L, D_FF, D_MODEL), D_FF),
    }

def first_block(x, c, w_ada, b_ada, norm1_w, w_in, q_norm_w, k_norm_w, w_pool, pool_scale,
              w_a_up, w_b_up, w_o, norm2_w, w_ff1, w_ff2):
    B, S, D = x.shape
    split_at = [POOL_WIDTH, POOL_WIDTH + SB_WIDTH, POOL_WIDTH + 2 * SB_WIDTH,
                POOL_WIDTH + 3 * SB_WIDTH, POOL_WIDTH + 3 * SB_WIDTH + D_MODEL]
    for l in range(DEPTH):
        mod = jax.nn.silu(c) @ w_ada[l] + b_ada[l]
        shift1, scale1, gate1, shift2, scale2, gate2 = jnp.split(mod, N_MOD, axis=-1)

        h = rms_norm(x, norm1_w[l]) * (1.0 + scale1[:, None]) + shift1[:, None]
        proj = h @ w_in[l]
        u_pool, q, k, v, g_a, g_b = jnp.split(proj, split_at, axis=-1)

        y_a = multiscale_pool(u_pool, w_pool[l], pool_scale[l]) @ w_a_up[l]

        q = rms_norm(q.reshape(B, S, SB_HEADS, SB_HEAD_DIM), q_norm_w[l])
        k = rms_norm(k.reshape(B, S, SB_HEADS, SB_HEAD_DIM), k_norm_w[l])
        v = v.reshape(B, S, SB_HEADS, SB_HEAD_DIM)
        y_b = stick_breaking_attention(q, k, v) @ w_b_up[l]

        merged = jax.nn.sigmoid(g_a) * y_a + jax.nn.sigmoid(g_b) * y_b
        x = x + gate1[:, None] * (merged @ w_o[l])

        h2 = rms_norm(x, norm2_w[l]) * (1.0 + scale2[:, None]) + shift2[:, None]
        f = jnp.square(jax.nn.relu(h2 @ w_ff1[l])) @ w_ff2[l]
        x = x + gate2[:, None] * f
    return x


DEPTH_2 = 2

N_MIXERS = 3
HEAD_DIM = 64
ROPE_DIM = HEAD_DIM // 4
ROPE_THETA = 500000.0
NORM_EPS = 1e-5

A_HEADS = D_MODEL // HEAD_DIM
A_KV_HEADS = A_HEADS // 8
A_GROUP = A_HEADS // A_KV_HEADS
A_WIDTH = A_HEADS * HEAD_DIM
A_KV_WIDTH = A_KV_HEADS * HEAD_DIM
A_IN = 2 * A_WIDTH + 2 * A_KV_WIDTH
A_WINDOW = 128
A_QBLOCK = 128

B_HEADS = D_MODEL // HEAD_DIM
B_KV_GROUPS = 4
B_GROUP = B_HEADS // B_KV_GROUPS
B_WIDTH = B_HEADS * HEAD_DIM
B_KV_WIDTH = B_KV_GROUPS * HEAD_DIM
B_N_BRANCH = 3
B_IN = 2 * B_WIDTH + 6 * B_KV_WIDTH + B_N_BRANCH * B_HEADS
CMP_BLOCK = 32
CMP_STRIDE = 16
CMP_HIDDEN = 4 * HEAD_DIM
SLC_BLOCK = 64
SLC_TOPK = 16
B_WINDOW = 512
B_QBLOCK = 64
WIN_QBLOCK = 128

C_WIDTH = D_MODEL
C_IN = 4 * C_WIDTH
CONV_WIDTH = 3

N_A = (DEPTH_2 + 2) // N_MIXERS
N_B = (DEPTH_2 + 1) // N_MIXERS
N_C = DEPTH_2 // N_MIXERS


def rmsnorm(x, g):
    xf = x.astype(jnp.float32)
    y = xf * lax.rsqrt(jnp.mean(xf * xf, axis=-1, keepdims=True) + NORM_EPS)
    return (y * g.astype(jnp.float32)).astype(x.dtype)

def rope_tables(positions):
    inv_freq = ROPE_THETA ** (-jnp.arange(0, ROPE_DIM, 2, dtype=jnp.float32) / ROPE_DIM)
    ang = positions.astype(jnp.float32)[..., None] * inv_freq
    return jnp.cos(ang)[:, :, None, :], jnp.sin(ang)[:, :, None, :]

def apply_rope(x, cos, sin):
    half = ROPE_DIM // 2
    x1 = x[..., :half].astype(jnp.float32)
    x2 = x[..., half:ROPE_DIM].astype(jnp.float32)
    r1 = x1 * cos - x2 * sin
    r2 = x2 * cos + x1 * sin
    return jnp.concatenate([r1.astype(x.dtype), r2.astype(x.dtype), x[..., ROPE_DIM:]], axis=-1)

def banded_attention(q, k, v, window, qblock, sinks=None):
    Bn, S, G, Hg, hd = q.shape
    nqb = S // qblock
    span = window + qblock
    scale = hd ** -0.5
    k_pad = jnp.pad(k, ((0, 0), (window, 0), (0, 0), (0, 0)))
    v_pad = jnp.pad(v, ((0, 0), (window, 0), (0, 0), (0, 0)))
    q_blocks = q.reshape(Bn, nqb, qblock, G, Hg, hd).swapaxes(0, 1)
    starts = jnp.arange(nqb, dtype=jnp.int32) * qblock
    rel = jnp.arange(qblock)[:, None] - jnp.arange(span)[None, :] + window
    band = (rel >= 0) & (rel < window)

    def step(args):
        qb, s0 = args
        kb = lax.dynamic_slice_in_dim(k_pad, s0, span, axis=1).astype(jnp.float32)
        vb = lax.dynamic_slice_in_dim(v_pad, s0, span, axis=1).astype(jnp.float32)
        s = jnp.einsum('bqghd,bkgd->bghqk', qb.astype(jnp.float32), kb) * scale
        valid = band & ((s0 - window + jnp.arange(span)) >= 0)[None, :]
        s = jnp.where(valid, s, -jnp.inf)
        if sinks is None:
            p = jax.nn.softmax(s, axis=-1)
        else:
            sk = sinks.astype(jnp.float32)[None, :, :, None, None]
            m = jnp.maximum(jnp.max(s, axis=-1, keepdims=True), sk)
            e = jnp.exp(s - m)
            p = e / (jnp.sum(e, axis=-1, keepdims=True) + jnp.exp(sk - m))
        o = jnp.einsum('bghqk,bkgd->bqghd', p, vb)
        return o.astype(q.dtype)

    o = lax.map(step, (q_blocks, starts))
    return o.swapaxes(0, 1).reshape(Bn, S, G, Hg, hd)

def mixer_a(h, w_in, sinks, w_out, cos, sin):
    Bn, S, _ = h.shape
    proj = h @ w_in
    q, k, v, z = jnp.split(proj, [A_WIDTH, A_WIDTH + A_KV_WIDTH, A_WIDTH + 2 * A_KV_WIDTH], axis=-1)
    q = apply_rope(q.reshape(Bn, S, A_HEADS, HEAD_DIM), cos, sin).reshape(Bn, S, A_KV_HEADS, A_GROUP, HEAD_DIM)
    k = apply_rope(k.reshape(Bn, S, A_KV_HEADS, HEAD_DIM), cos, sin)
    v = v.reshape(Bn, S, A_KV_HEADS, HEAD_DIM)
    o = banded_attention(q, k, v, A_WINDOW, A_QBLOCK, sinks.reshape(A_KV_HEADS, A_GROUP))
    o = o.reshape(Bn, S, A_WIDTH)
    return (o * jax.nn.silu(z)) @ w_out

def compress(k, pos, w1, w2):
    Bn, S, G, hd = k.shape
    nc = (S - CMP_BLOCK) // CMP_STRIDE + 1
    idx = np.arange(nc)[:, None] * CMP_STRIDE + np.arange(CMP_BLOCK)[None, :]
    blocks = k[:, idx] + pos[None, None, :, None, :]
    blocks = jnp.moveaxis(blocks, 3, 2).reshape(Bn, nc, G, CMP_BLOCK * hd)
    return jax.nn.gelu(blocks @ w1) @ w2

def nsa_cmp_slc(q, kcmp, vcmp, ks, vs):
    Bn, S, G, Hg, hd = q.shape
    nc = kcmp.shape[1]
    nsel = S // SLC_BLOCK
    n_top = min(SLC_TOPK, nsel)
    nqb = S // B_QBLOCK
    scale = hd ** -0.5
    c_start = np.arange(nc) * CMP_STRIDE
    c_end = c_start + CMP_BLOCK
    s_start = np.arange(nsel) * SLC_BLOCK
    s_end = s_start + SLC_BLOCK
    overlap = np.clip(np.minimum(c_end[:, None], s_end[None, :]) - np.maximum(c_start[:, None], s_start[None, :]), 0, None)
    overlap = jnp.asarray(overlap / CMP_BLOCK, jnp.float32)
    c_last = jnp.asarray(c_end - 1, jnp.int32)
    kcmp_f = kcmp.astype(jnp.float32)
    vcmp_f = vcmp.astype(jnp.float32)
    ks_blk = ks.reshape(Bn, nsel, SLC_BLOCK, G, hd).transpose(0, 1, 3, 2, 4)
    vs_blk = vs.reshape(Bn, nsel, SLC_BLOCK, G, hd).transpose(0, 1, 3, 2, 4)
    q_blocks = q.reshape(Bn, nqb, B_QBLOCK, G, Hg, hd).swapaxes(0, 1)
    starts = jnp.arange(nqb, dtype=jnp.int32) * B_QBLOCK
    bi = jnp.arange(Bn)[:, None, None, None]
    gi = jnp.arange(G)[None, None, :, None]
    blk = jnp.arange(nsel)

    def step(args):
        qb, s0 = args
        t = s0 + jnp.arange(B_QBLOCK)
        qf = qb.astype(jnp.float32)
        sc = jnp.einsum('bqghd,bcgd->bghqc', qf, kcmp_f) * scale
        sc = jnp.where(c_last[None, :] <= t[:, None], sc, -jnp.inf)
        m = jnp.max(sc, axis=-1, keepdims=True)
        m = jnp.where(jnp.isfinite(m), m, 0.0)
        e = jnp.exp(sc - m)
        p_cmp = e / jnp.maximum(jnp.sum(e, axis=-1, keepdims=True), 1e-30)
        o_cmp = jnp.einsum('bghqc,bcgd->bqghd', p_cmp, vcmp_f)
        imp = jnp.einsum('bghqc,cn->bgqn', p_cmp, overlap)
        cur = t // SLC_BLOCK
        forced = (blk[None, :] == 0) | (blk[None, :] == cur[:, None]) | (blk[None, :] == cur[:, None] - 1)
        future = blk[None, :] * SLC_BLOCK > t[:, None]
        imp = jnp.where(forced, jnp.inf, imp)
        imp = jnp.where(future, -jnp.inf, imp)
        _, sel = lax.top_k(imp, n_top)
        sel = sel.transpose(0, 2, 1, 3)
        kg = ks_blk[bi, sel, gi].astype(jnp.float32)
        vg = vs_blk[bi, sel, gi].astype(jnp.float32)
        ss = jnp.einsum('bqghd,bqgnld->bghqnl', qf, kg) * scale
        kpos = sel[..., None] * SLC_BLOCK + jnp.arange(SLC_BLOCK)
        valid = (kpos <= t[None, :, None, None, None]).transpose(0, 2, 1, 3, 4)[:, :, None]
        ss = jnp.where(valid, ss, -jnp.inf)
        shp = ss.shape
        p_slc = jax.nn.softmax(ss.reshape(shp[:4] + (n_top * SLC_BLOCK,)), axis=-1).reshape(shp)
        o_slc = jnp.einsum('bghqnl,bqgnld->bqghd', p_slc, vg)
        return o_cmp.astype(q.dtype), o_slc.astype(q.dtype)

    o_cmp, o_slc = lax.map(step, (q_blocks, starts))
    o_cmp = o_cmp.swapaxes(0, 1).reshape(Bn, S, G, Hg, hd)
    o_slc = o_slc.swapaxes(0, 1).reshape(Bn, S, G, Hg, hd)
    return o_cmp, o_slc

def mixer_b(h, w_in, kc_pos, kc_w1, kc_w2, vc_pos, vc_w1, vc_w2, w_out, cos, sin):
    Bn, S, _ = h.shape
    proj = h @ w_in
    cuts = [B_WIDTH + i * B_KV_WIDTH for i in range(7)] + [B_WIDTH + 6 * B_KV_WIDTH + B_N_BRANCH * B_HEADS]
    q, kc, vc, ks, vs, kw, vw, gates, z = jnp.split(proj, cuts, axis=-1)
    q = apply_rope(q.reshape(Bn, S, B_HEADS, HEAD_DIM), cos, sin).reshape(Bn, S, B_KV_GROUPS, B_GROUP, HEAD_DIM)
    kv_shape = (Bn, S, B_KV_GROUPS, HEAD_DIM)
    ks = apply_rope(ks.reshape(kv_shape), cos, sin)
    kw = apply_rope(kw.reshape(kv_shape), cos, sin)
    kcmp = compress(kc.reshape(kv_shape), kc_pos, kc_w1, kc_w2)
    vcmp = compress(vc.reshape(kv_shape), vc_pos, vc_w1, vc_w2)
    o_cmp, o_slc = nsa_cmp_slc(q, kcmp, vcmp, ks, vs.reshape(kv_shape))
    o_win = banded_attention(q, kw, vw.reshape(kv_shape), B_WINDOW, WIN_QBLOCK)
    g = jax.nn.sigmoid(gates.astype(jnp.float32)).reshape(Bn, S, B_N_BRANCH, B_KV_GROUPS, B_GROUP, 1)
    o = (g[:, :, 0] * o_cmp.astype(jnp.float32) + g[:, :, 1] * o_slc.astype(jnp.float32)
         + g[:, :, 2] * o_win.astype(jnp.float32)).astype(h.dtype)
    o = o.reshape(Bn, S, B_WIDTH)
    return (o * jax.nn.silu(z)) @ w_out

def mixer_c(h, w_in, conv_w, w_out):
    u, b_gate, c_gate, z = jnp.split(h @ w_in, 4, axis=-1)
    v = c_gate * u
    y = lax.conv_general_dilated(v, conv_w[:, None, :], window_strides=(1,), padding=[(CONV_WIDTH - 1, 0)],
                                 dimension_numbers=('NWC', 'WIO', 'NWC'), feature_group_count=C_WIDTH)
    y = b_gate * y
    return (y * jax.nn.silu(z)) @ w_out

def second_inputs(seed: int = 0) -> dict:
    key = jax.random.key(seed)
    ks = jax.random.split(key, 20)

    def dense(k, shape, fan_in):
        return jax.random.normal(k, shape, jnp.float32) * fan_in ** -0.5

    x = jax.random.normal(ks[0], (BATCH, SEQ, D_MODEL), jnp.float32)
    positions = (jnp.arange(SEQ, dtype=jnp.int32)[None, :]
                 + jax.random.randint(ks[1], (BATCH, 1), 0, 1024, dtype=jnp.int32))
    norm_w = 1.0 + 0.02 * jax.random.normal(ks[2], (DEPTH_2, D_MODEL), jnp.float32)
    final_norm_w = 1.0 + 0.02 * jax.random.normal(ks[3], (D_MODEL,), jnp.float32)
    a_w_in = dense(ks[4], (N_A, D_MODEL, A_IN), D_MODEL)
    a_sinks = jax.random.normal(ks[5], (N_A, A_HEADS), jnp.float32)
    a_w_out = dense(ks[6], (N_A, A_WIDTH, D_MODEL), A_WIDTH)
    b_w_in = dense(ks[7], (N_B, D_MODEL, B_IN), D_MODEL)
    b_cmp_k_pos = 0.1 * jax.random.normal(ks[8], (N_B, CMP_BLOCK, HEAD_DIM), jnp.float32)
    b_cmp_k_w1 = dense(ks[9], (N_B, CMP_BLOCK * HEAD_DIM, CMP_HIDDEN), CMP_BLOCK * HEAD_DIM)
    b_cmp_k_w2 = dense(ks[10], (N_B, CMP_HIDDEN, HEAD_DIM), CMP_HIDDEN)
    b_cmp_v_pos = 0.1 * jax.random.normal(ks[11], (N_B, CMP_BLOCK, HEAD_DIM), jnp.float32)
    b_cmp_v_w1 = dense(ks[12], (N_B, CMP_BLOCK * HEAD_DIM, CMP_HIDDEN), CMP_BLOCK * HEAD_DIM)
    b_cmp_v_w2 = dense(ks[13], (N_B, CMP_HIDDEN, HEAD_DIM), CMP_HIDDEN)
    b_w_out = dense(ks[14], (N_B, B_WIDTH, D_MODEL), B_WIDTH)
    c_w_in = dense(ks[15], (N_C, D_MODEL, C_IN), D_MODEL)
    c_conv_w = dense(ks[16], (N_C, CONV_WIDTH, C_WIDTH), CONV_WIDTH)
    c_w_out = dense(ks[17], (N_C, C_WIDTH, D_MODEL), C_WIDTH)
    return {"x": x, "positions": positions, "norm_w": norm_w, "final_norm_w": final_norm_w,
            "a_w_in": a_w_in, "a_sinks": a_sinks, "a_w_out": a_w_out,
            "b_w_in": b_w_in, "b_cmp_k_pos": b_cmp_k_pos, "b_cmp_k_w1": b_cmp_k_w1, "b_cmp_k_w2": b_cmp_k_w2,
            "b_cmp_v_pos": b_cmp_v_pos, "b_cmp_v_w1": b_cmp_v_w1, "b_cmp_v_w2": b_cmp_v_w2, "b_w_out": b_w_out,
            "c_w_in": c_w_in, "c_conv_w": c_conv_w, "c_w_out": c_w_out}

def second_block(x, positions, norm_w, final_norm_w, a_w_in, a_sinks, a_w_out,
              b_w_in, b_cmp_k_pos, b_cmp_k_w1, b_cmp_k_w2, b_cmp_v_pos, b_cmp_v_w1, b_cmp_v_w2, b_w_out,
              c_w_in, c_conv_w, c_w_out):
    cos, sin = rope_tables(positions)
    for i in range(DEPTH_2):
        h = rmsnorm(x, norm_w[i])
        kind, j = i % N_MIXERS, i // N_MIXERS
        if kind == 0:
            out = mixer_a(h, a_w_in[j], a_sinks[j], a_w_out[j], cos, sin)
        elif kind == 1:
            out = mixer_b(h, b_w_in[j], b_cmp_k_pos[j], b_cmp_k_w1[j], b_cmp_k_w2[j],
                          b_cmp_v_pos[j], b_cmp_v_w1[j], b_cmp_v_w2[j], b_w_out[j], cos, sin)
        else:
            out = mixer_c(h, c_w_in[j], c_conv_w[j], c_w_out[j])
        x = x + out.astype(x.dtype)
    return rmsnorm(x, final_norm_w)


def setup_inputs(seed=0):
    out = dict(first_inputs(seed))
    for name, value in second_inputs(seed + 1).items():
        if name != "x":
            out[name + "_2"] = value
    return out


def reference(
    x, c, w_ada, b_ada, norm1_w, w_in, q_norm_w, k_norm_w, w_pool, pool_scale, w_a_up, w_b_up,
    w_o, norm2_w, w_ff1, w_ff2, positions_2, norm_w_2, final_norm_w_2, a_w_in_2, a_sinks_2,
    a_w_out_2, b_w_in_2, b_cmp_k_pos_2, b_cmp_k_w1_2, b_cmp_k_w2_2, b_cmp_v_pos_2, b_cmp_v_w1_2,
    b_cmp_v_w2_2, b_w_out_2, c_w_in_2, c_conv_w_2, c_w_out_2,
):
    x = first_block(
        x, c, w_ada, b_ada, norm1_w, w_in, q_norm_w, k_norm_w, w_pool, pool_scale, w_a_up,
        w_b_up, w_o, norm2_w, w_ff1, w_ff2,
    )
    return second_block(
        x, positions_2, norm_w_2, final_norm_w_2, a_w_in_2, a_sinks_2, a_w_out_2, b_w_in_2,
        b_cmp_k_pos_2, b_cmp_k_w1_2, b_cmp_k_w2_2, b_cmp_v_pos_2, b_cmp_v_w1_2, b_cmp_v_w2_2,
        b_w_out_2, c_w_in_2, c_conv_w_2, c_w_out_2,
    )


_drawn_inputs = setup_inputs


def setup_inputs(seed=0):
    import zlib

    import numpy as np

    out = dict(_drawn_inputs(seed))
    spreads = {}
    factors = {'norm1_w': 5.214,
     'q_norm_w': 8.0,
     'k_norm_w': 8.0,
     'pool_scale': 3.714,
     'norm_w_2': 8.0,
     'final_norm_w_2': 7.83,
     'a_sinks_2': 4.588,
     'b_cmp_k_pos_2': 8.0,
     'b_cmp_v_pos_2': 16.175}
    for name, (base, spread) in spreads.items():
        noise = np.random.default_rng([zlib.crc32(name.encode()), seed]).standard_normal(out[name].shape)
        drawn = base * np.exp(spread * noise) if base else spread * noise
        out[name] = __import__('jax').numpy.asarray(drawn.astype(out[name].dtype))
    for name, factor in factors.items():
        out[name] = (out[name] * factor).astype(out[name].dtype)
    return out
```

```python
from contextlib import ExitStack, contextmanager

import numpy as np
import concourse.bass as bass
from concourse import mybir
from concourse.alu_op_type import AluOpType as ALU

F32 = mybir.dt.float32
F32R = mybir.dt.float32r
I32 = mybir.dt.int32
ACT = mybir.ActivationFunctionType
AX = mybir.AxisListType.X
ds = bass.ds

P = 128
SEQ = 256
NT = SEQ // P
D = 2048
KT = D // P
CH = 512
UK = 4
RAW = 4
SK = 2
HALF = UK // SK
SPL = 4
AHEAD = 3
POOL_W = 1024
WINDOWS = (2, 4, 8, 16)
SBH = 8
HD = 64
GROUPS = 4
GH = 8
NC = (SEQ - 32) // 16 + 1
D_FF = 4 * D
NEG = -1.0e30
AC = 256
AK = 2
ADA_RING = 4


class Sem:

    def __init__(self, handle, name):
        self.h, self.name, self.n, self.per = handle, name, 0, 0


class Program:

    def __init__(self, nc, ctx, per_loop):
        self.nc, self.ctx, self.per_loop = nc, ctx, per_loop
        self.sems, self.loops, self.i, self.seen = [], 0, None, {}

    def sem(self, name):
        s = Sem(self.ctx.enter_context(self.nc.semaphore(name)), name)
        self.sems.append(s)
        return s

    def sig(self, inst, s, k=1):
        inst.then_inc(s.h, k)
        s.n += k
        return (s, s.n)

    def now(self, s):
        return (s, s.n)

    def wait(self, eng, *tokens):
        for s, n in tokens:
            key = (eng.engine, s.name)
            if (n <= 0 and s.per == 0) or self.seen.get(key, -10**9) >= n:
                continue
            self.seen[key] = n
            eng.wait_ge(s.h, self.i * s.per + n if s.per else n)

    @contextmanager
    def loop(self, n):
        k = self.loops
        self.loops += 1
        per = self.per_loop.get(k, {})
        start = {}
        for s in self.sems:
            s.per = per.get(s.name, 0)
            start[s.name] = s.n
        with self.nc.Fori(0, n) as i:
            self.i, self.seen = i, {}
            yield i
        self.per_loop[k] = {s.name: s.n - start[s.name] for s in self.sems}
        for s in self.sems:
            s.n = start[s.name] + n * self.per_loop[k][s.name]
            s.per = 0
        self.i, self.seen = None, {}


def build(nc, t, per_loop):
    with ExitStack() as ctx:
        body(nc, t, Program(nc, ctx, per_loop), ctx)


def body(nc, t, p, ctx):
    S, A, V, G, T = nc.sync, nc.scalar, nc.vector, nc.gpsimd, nc.tensor
    sig, wait, now = p.sig, p.wait, p.now

    def sb(name, shape, dt=F32, c=None):
        return (c or ctx).enter_context(nc.sbuf_tensor(name, shape, dt))

    sA, sV, sG, sT = (p.sem(n) for n in ("act_step", "vec_step", "pool_step", "pe_step"))
    raw_in = [p.sem(f"raw_landed{i}") for i in range(RAW)]
    high_done, low_done = p.sem("high_done"), p.sem("low_done")
    unit_done = p.sem("unit_done")
    pro_done = [p.sem(f"prologue_unit_done_{e}") for e in ("pe", "vec", "pool")]
    ada_in = [p.sem(f"ada_landed{i}") for i in range(ADA_RING)]
    ada_done = p.sem("ada_done")
    c_in, x_in = p.sem("c_landed"), p.sem("x_landed")
    small_in, pool_in, gate_in = p.sem("small_landed"), p.sem("pool_w_landed"), p.sem("gate_bias_landed")
    kv_in, end_in, out_in = p.sem("kv_w_landed"), p.sem("final_w_landed"), p.sem("out_stored")
    loads = p.sem("loads_begun")
    evac = [p.sem("pair0_read"), p.sem("pair1_read")]

    raw = sb("raw", [P, RAW, UK, CH])
    WH = sb("w_high", [P, SPL, SK, CH], F32R)
    WL = sb("w_low", [P, SPL, SK, CH], F32R)
    ada_w = sb("ada_w", [P, ADA_RING, AK, AC])
    x = sb("x", [P, NT, D])
    AH = sb("act_a_high", [P, KT, SEQ], F32R)
    AL = sb("act_a_low", [P, KT, SEQ], F32R)
    gate_b = sb("gate_b", [P, D])
    ident = sb("ident", [P, P])
    ones = sb("ones", [P, P])
    cols1 = sb("cols1", [P, P])
    cols2 = sb("cols2", [P, P])
    mod1 = sb("mod1", [P, 2, KT])
    mod2 = sb("mod2", [P, 2, KT])
    cT = sb("cT", [P, KT])
    ss = sb("sums_for_rms", [P, 16])
    rs = sb("inverse_rms", [P, 16])
    ssq = sb("sums_of_squares", [P, NT, D // CH])
    mhalf = sb("minus_half", [P, 16])
    ada_acc = sb("ada_acc", [P, 2, AC])

    banks = ctx.enter_context(nc.psum_tensor("banks", [P, 8, CH], F32))
    pair = [banks[:, 0:2, :], banks[:, 2:4, :]]

    def bank(b):
        return banks[:, 4 + b, :]

    last = {}

    def all_settled():
        last.clear()
        last["*"] = [now(s) for s in (sA, sV, sG, sT, *evac)]
        last["ada_acc0"], last["ada_acc1"] = [now(sT)], [now(sT)]
        last["pair0"], last["pair1"] = [now(evac[0])], [now(evac[1])]

    last["*"] = []

    def scope():
        all_settled()
        for eng in (A, V, G):
            wait(eng, *last["*"])
        return ExitStack()

    def take(eng, name):
        wait(eng, *last.get(name, last["*"]))
        last[name] = []

    def used(name, token):
        last.setdefault(name, []).append(token)
        return token

    cnt = {"load": 0, "split": 0, "mm": 0, "ada_load": 0, "ada_use": 0, "piece": 0}
    pro_cnt = {"load": 0, "use": 0}
    newest, ada_step = [None], [None]
    PRO = 2 * D // CH * (KT // UK)

    @contextmanager
    def loop(n):
        before, before_p = dict(cnt), dict(pro_cnt)
        with p.loop(n) as i:
            all_settled()
            yield i
        for count, was in ((cnt, before), (pro_cnt, before_p)):
            for k in count:
                count[k] = was[k] + n * (count[k] - was[k])
        all_settled()

    V.sem_inc(low_done.h, RAW * HALF)
    T.sem_inc(unit_done.h, SPL)
    V.sem_inc(ada_done.h, ADA_RING)
    V.sem_inc(evac[0].h, 1)
    V.sem_inc(evac[1].h, 1)
    low_done.n, unit_done.n, ada_done.n, evac[0].n, evac[1].n = RAW * HALF, SPL, ADA_RING, 1, 1

    def load_unit(src, k=UK, n=CH):
        u = cnt["load"]
        cnt["load"] += 1
        wait(S, (low_done, HALF * (u + 1)))
        S.sem_inc(loads.h, 1)
        dst = raw[:, u % RAW, :, :]
        if n != CH:
            dst = dst.rearrange("p a (x b) -> p (a x) b", x=k // UK)[:, :, 0:n]
        sig(S.dma_start(dst, src), raw_in[u % RAW], 16)

    def split_part():
        u = cnt["split"]
        cnt["split"] += 1
        r, sl, h = u // HALF % RAW, slice(u % HALF * SK, (u % HALF + 1) * SK), u % SPL
        wait(A, (raw_in[r], 16 * ((PRO + u // HALF) // RAW + 1)), (unit_done, u + 1))
        sig(A.copy(WH[:, h, :, :], raw[:, r, sl, :]), high_done)
        wait(V, (high_done, u + 1))
        sig(V.tensor_tensor(WL[:, h, :, :], raw[:, r, sl, :], WH[:, h, :, :].bitcast(F32), ALU.subtract), low_done)

    def ktile(b, k, nk, stat, kk, end, width=CH):
        u = cnt["mm"]
        wait(T, (low_done, RAW * HALF + u + 1))
        wh, wl = WH[:, u % SPL, :, :], WL[:, u % SPL, :, :]
        if width == CH:
            wh, wl = wh[:, kk, :], wl[:, kk, :]
        else:
            wh, wl = (w.rearrange("p a (x b) -> p (a x) b", b=P)[:, kk, 0:width] for w in (wh, wl))
        for tt in range(NT):
            out = pair[b][:, tt, 0:width]
            xh, xl = (s[:, k, tt * P:(tt + 1) * P] for s in stat)
            T.matmul(out, xh, wh, start=(k == 0), stop=False)
            T.matmul(out, xh, wl, start=False, stop=False)
            mm = T.matmul(out, xl, wh, start=False, stop=(k == nk - 1))
        if end:
            cnt["mm"] += 1
            sig(mm, unit_done)

    def chunk(b, w, col, stat, row=0, nk=KT, hooks=None, final=False, ada=None):
        hooks = hooks or {}
        for u in range(nk // UK):
            r = row + u * UK * P
            load_unit(w[ds(r, UK * P), ds(col, CH)].rearrange("(k p) n -> p k n", p=P))
        if ada is not None:
            ada_load(ada, 0, ADA_RING)
        take(T, f"pair{b}")
        for k in range(nk):
            if k % SK == 0 and not (final and k >= nk - AHEAD * SK):
                split_part()
            if ada is not None:
                a0, a1 = k * KT // nk, (k + 1) * KT // nk
                ada_tiles(a0, a1)
                ada_load(ada, *(min(a // AK + ADA_RING, KT // AK) for a in (a0, a1)))
            for fn in hooks.get(k, ()):
                fn()
            ktile(b, k, nk, stat, k % SK, k % SK == SK - 1)
        return now(unit_done)

    def read_pair(b, inst):
        return used(f"pair{b}", sig(inst, evac[b]))

    def ada_load(col, q0, q1):
        for q in range(q0, q1):
            u = cnt["ada_load"]
            cnt["ada_load"] += 1
            wait(G, (ada_done, u + 1))
            sig(G.dma_start(ada_w[:, u % ADA_RING, :, :], t["w_ada"][0, q * AK * P:(q + 1) * AK * P, ds(col, AC)]
                            .rearrange("(k p) n -> p k n", p=P)), ada_in[u % ADA_RING], 16)

    def ada_tiles(a0, a1):
        n = cnt["piece"] % 2
        acc = ada_acc[:, n, :]
        for a in range(a0, a1):
            u = cnt["ada_use"]
            w, c = ada_w[:, u % ADA_RING, a % AK, :], cT[:, a:a + 1]
            wait(V, (ada_in[u % ADA_RING], 16 * (u // ADA_RING + 1)))
            if a == 0:
                take(V, f"ada_acc{n}")
                step = V.tensor_scalar(acc, w, c, None, ALU.mult)
            else:
                wait(V, ada_step[0])
                step = V.scalar_tensor_tensor(out=acc, in0=w, scalar=c, in1=acc, op0=ALU.mult, op1=ALU.add)
            ada_step[0] = sig(step, ada_done if a % AK == AK - 1 else sV)
            cnt["ada_use"] += a % AK == AK - 1
        if a1 == KT:
            newest[0] = (n, now(ada_done))
            cnt["piece"] += 1

    def ada_piece():
        return newest[0]

    def ada_columns(done, dst, b):
        n, done = done
        take(T, f"bank{b}")
        wait(T, done)
        for j in range(AC // P):
            mm = T.matmul(bank(b)[:, j:j + 1], ada_acc[:, n, j * P:(j + 1) * P], ones[:, 0:1], start=True, stop=True)
        m = used(f"ada_acc{n}", sig(mm, sT))
        wait(V, m)
        used(f"bank{b}", sig(V.tensor_copy(dst, bank(b)[:, 0:AC // P]), sV))

    def ada_rows(done, col, b):
        n, done = done
        take(T, f"bank{b}")
        wait(T, done)
        m = used(f"ada_acc{n}", sig(T.matmul(bank(b)[:, 0:AC], ones[:, :], ada_acc[:, n, :], start=True, stop=True), sT))
        wait(V, m)
        g = gate_b[:, ds(col, AC)]
        used(f"bank{b}", used("gate_b", sig(V.tensor_tensor(g, bank(b)[:, 0:AC], g, ALU.add), sV)))

    def rsqrt(n, mean, eps, *ready):
        wait(V, *ready)
        a = sig(V.tensor_scalar(ss[:, 0:n], ss[:, 0:n], 1.0 / mean, eps, ALU.mult, ALU.add), sV)
        wait(G, a)
        take(G, "rs")
        return used("ss", sig(G.tensor_tensor(rs[:, 0:n], ss[:, 0:n], mhalf[:, 0:n], ALU.pow), sG))

    def transposes(b, src, c0, ready):
        take(T, f"bank{b}")
        wait(T, *ready)
        for j in range(2):
            for tt in range(NT):
                tr = T.transpose(bank(b)[:, j * SEQ + tt * P:j * SEQ + (tt + 1) * P],
                                 src[:, tt, c0 + j * P:c0 + (j + 1) * P], ident[:, :])
        return sig(tr, sT)

    def turn(src, name, ready, dst, k0, b2=(0, 1)):
        for half in range(2):
            b = b2[half]
            m = used(name, transposes(b, src, 2 * half * P, ready))
            H, L = dst[0][:, ds(k0 + 2 * half, 2), :], dst[1][:, ds(k0 + 2 * half, 2), :]
            ps = bank(b).rearrange("p (a c) -> p a c", c=SEQ)
            wait(A, m)
            h = sig(A.copy(H, ps), sA)
            wait(V, h)
            l = used(f"bank{b}", sig(V.tensor_tensor(L, ps, H.bitcast(F32), ALU.subtract), sV))
        return l

    def a_load(dst, src, s, **kw):
        return sig(A.dma_start(dst, src, **kw), s, 16)

    attn = ExitStack()
    qT = sb("qT", [P, SBH, SEQ], c=attn)
    merged = sb("merged", [P, NT, D], c=attn)
    p0 = ExitStack()
    rows1 = sb("rows1", [P, P], c=p0)
    rows2 = sb("rows2", [P, P], c=p0)
    xT = sb("xT", [P, KT, SEQ], c=p0)
    xn0 = sb("xn0", [P, NT, D], c=p0)
    tmp0 = sb("tmp0", [P, 2, SEQ], c=p0)
    acc_v = sb("ada_acc_vec", [P, 2, CH], c=p0)
    acc_g = sb("ada_acc_pool", [P, 2, CH], c=p0)
    row_s = sb("ada_row", [1, 2, CH], c=p0)
    c_rows = a_load(rows1[0:16, :], t["c"].rearrange("a (r q) -> (a r) q", q=P), c_in)
    x_loaded = a_load(x[:, :, :], t["x"][0].rearrange("(a q) d -> q a d", q=P), x_in)
    a_load(rows1[16:32, :], t["norm1_w"].rearrange("a (r q) -> (a r) q", q=P), small_in)
    a_load(rows1[32:128, :], t["b_ada"].rearrange("a (r q) -> (a r) q", q=P), small_in)
    at, r2 = {}, 0
    for name, n, src in (
        ("norm2", KT, t["norm2_w"].rearrange("a (r q) -> (a r) q", q=P)),
        ("norm_2", 2 * KT, t["norm_w_2"].rearrange("a (r q) -> (a r) q", q=P)),
        ("pool_scale", 8, t["pool_scale"].rearrange("a (r q) -> (a r) q", q=P)),
        ("q_norm", 1, t["q_norm_w"]),
        ("k_norm", 1, t["k_norm_w"]),
        ("pos_k", 16, t["b_cmp_k_pos_2"].rearrange("a (r q) d -> (a r) (q d)", q=2)),
        ("pos_v", 16, t["b_cmp_v_pos_2"].rearrange("a (r q) d -> (a r) (q d)", q=2)),
    ):
        a_load(rows2[r2:r2 + n, :], src, small_in)
        at[name] = r2
        r2 += n
    small = now(small_in)
    bias_in = a_load(gate_b[:, :], t["b_ada"][0:1, 2 * D:3 * D].partition_broadcast(P), gate_in)

    g = sig(G.memset(ident[:, :], 0.0), sG)
    G.memset(mhalf[:, :], -0.5)
    sig(G.memset(ones[:, :], 1.0), sG)
    wait(G, g)
    consts = sig(G.affine_select(out=ident[:, :], in_=ident[:, :], compare_op=ALU.not_equal, fill=1.0, base=0,
                                 pattern=[[-1, P]], channel_multiplier=1), sG)

    for e, s_ in zip((T, V, G), pro_done):
        e.sem_inc(s_.h, RAW)
        s_.n = RAW
    def prologue_chunk(col, n):
        for u in range(KT // UK):
            w = pro_cnt["load"]
            pro_cnt["load"] += 1
            wait(S, *((s_, w + 1) for s_ in pro_done))
            S.sem_inc(loads.h, 1)
            sig(S.dma_start(raw[:, w % RAW, :, :], t["w_ada"][0, u * UK * P:(u + 1) * UK * P, ds(col * CH, CH)]
                            .rearrange("(k p) n -> p k n", p=P)), raw_in[w % RAW], 16)
        row = bank(2 + n)[0:1, :]
        take(T, f"bank{2 + n}")
        take(V, f"acc_v{n}")
        take(G, f"acc_g{n}")
        for u in range(KT // UK):
            w = pro_cnt["use"]
            pro_cnt["use"] += 1
            for eng in (T, V, G):
                wait(eng, (raw_in[w % RAW], 16 * (w // RAW + 1)))
            r, k = raw[:, w % RAW, :, :], u * UK
            sig(T.matmul(row, cT[:, k:k + 1], r[:, 0, :], start=(u == 0), stop=False), pro_done[0])
            for kk in (1, 2):
                if (u, kk) == (0, 1):
                    st = V.tensor_scalar(acc_v[:, n, :], r[:, kk, :], cT[:, k + kk:k + kk + 1], None, ALU.mult)
                else:
                    wait(V, v)
                    st = V.scalar_tensor_tensor(out=acc_v[:, n, :], in0=r[:, kk, :], scalar=cT[:, k + kk:k + kk + 1],
                                                in1=acc_v[:, n, :], op0=ALU.mult, op1=ALU.add)
                v = sig(st, sV if kk == 1 else pro_done[1])
            cb = cT[:, k + 3:k + 4].broadcast_to([P, CH])
            if u == 0:
                g = sig(G.tensor_tensor(acc_g[:, n, :], r[:, 3, :], cb, ALU.mult), pro_done[2])
            else:
                g = sig(G.tensor_tensor(r[:, 3, :], r[:, 3, :], cb, ALU.mult), sG)
                wait(G, g)
                g = sig(G.tensor_tensor(acc_g[:, n, :], acc_g[:, n, :], r[:, 3, :], ALU.add), pro_done[2])
            wait(G, g)
        wait(T, v)
        T.matmul(row, ones[:, 0:1], acc_v[:, n, :], start=False, stop=False)
        wait(T, g)
        m = sig(T.matmul(row, ones[:, 0:1], acc_g[:, n, :], start=False, stop=True), sT)
        used(f"acc_v{n}", m)
        used(f"acc_g{n}", m)
        take(A, f"row_s{n}")
        wait(A, m)
        a = used(f"bank{2 + n}", sig(A.copy(row_s[0:1, n, :], row), sA))
        wait(T, a)
        for j in range(CH // P):
            mm = T.matmul(banks[:, 0, ds(col * 4 + j, 1)], row_s[0:1, n, j * P:(j + 1) * P], ones[0:1, 0:1],
                          start=True, stop=True)
        used(f"row_s{n}", sig(mm, sT))

    wait(T, consts, c_rows)
    m = sig(T.transpose(bank(0)[:, 0:16], rows1[0:16, :], ident[0:16, 0:16]), sT)
    wait(V, m)
    v = used("bank0", sig(V.tensor_copy(cols1[:, 0:16], bank(0)[:, 0:16]), sV))
    wait(A, v)
    a = sig(A.activation(cT[:, :], cols1[:, 0:KT], ACT.Tanh, scale=0.5), sA)
    wait(V, a, v)
    v = sig(V.scalar_tensor_tensor(out=cT[:, :], in0=cT[:, :], scalar=1.0, in1=cols1[:, 0:KT],
                                   op0=ALU.add, op1=ALU.mult), sV)
    wait(V, v)
    cT_done = sig(V.tensor_scalar(cT[:, :], cT[:, :], 0.5, None, ALU.mult), sV)
    wait(T, cT_done)
    wait(G, cT_done)

    wait(A, x_loaded)
    for tt in range(NT):
        a = sig(A.activation(xn0[:, tt, :], x[:, tt, :], ACT.Square, accum_out=ss[:, tt:tt + 1]), sA)
    r = rsqrt(NT, D, 1e-6, a)
    wait(A, r, a)
    for tt in range(NT):
        xn_done = sig(A.activation(xn0[:, tt, :], x[:, tt, :], ACT.Copy, scale=rs[:, tt:tt + 1]), sA)
    all_settled()

    with loop(2) as i:
        for n in range(2):
            prologue_chunk(2 * i + n, n)

    wait(T, small)
    take(T, "bank0")
    T.transpose(bank(0)[:, 0:P], rows1[:, :], ident[:, :])
    m = sig(T.transpose(bank(0)[:, P:P + r2], rows2[0:r2, :], ident[0:r2, 0:r2]), sT)
    wait(V, m)
    v = sig(V.tensor_copy(cols1[:, :], bank(0)[:, 0:P]), sV)
    used("bank0", sig(V.tensor_copy(cols2[:, 0:r2], bank(0)[:, P:P + r2]), sV))
    for k in range(0, KT, 2):
        b = (k // 2) % 2
        m = transposes(b, xn0, k * P, [xn_done])
        wait(V, m)
        xT_done = used(f"bank{b}", sig(V.tensor_copy(xT[:, k:k + 2, :], bank(b).rearrange("p (a c) -> p a c", c=SEQ)), sV))

    with loop(2) as i:
        for n in range(2):
            prologue_chunk(2 * i + n + 4, n)

    w_in = t["w_in"][0]
    wait(S, *(now(s_) for s_ in pro_done))

    wait(V, now(sT))
    v = sig(V.tensor_tensor(mod1[:, :, :].rearrange("p a b -> p (a b)"), banks[:, 0, 0:2 * KT],
                            cols1[:, 32:32 + 2 * KT], ALU.add), sV)
    last["pair0"] = [v]
    wait(V, v)
    v = sig(V.scalar_tensor_tensor(out=mod1[:, 1, :], in0=mod1[:, 1, :], scalar=1.0, in1=cols1[:, KT:2 * KT],
                                   op0=ALU.add, op1=ALU.mult), sV)
    wait(V, v)

    def modulate(src, k, mod, dst, tmp, b=None):
        take(A, "tmp")
        for j in range(2):
            a = sig(A.activation(tmp[:, j, :], src[:, j, :], ACT.Identity, scale=mod[:, 1, k + j:k + j + 1],
                                 bias=mod[:, 0, k + j:k + j + 1]), sA)
        if b is not None:
            used(f"bank{b}", a)
        wait(A, a)
        h = sig(A.copy(dst[0][:, k:k + 2, :], tmp[:, :, :]), sA)
        wait(V, h)
        return used("tmp", sig(V.tensor_tensor(dst[1][:, k:k + 2, :], tmp[:, :, :], dst[0][:, k:k + 2, :].bitcast(F32),
                                               ALU.subtract), sV))

    wait(A, xT_done, v)
    split_k = {}

    def modulate_step(m):
        split_k[m] = modulate(xT[:, 2 * m:2 * m + 2, :], 2 * m, mod1, (AH, AL), tmp0)

    modulate_step(0)
    modulate_step(1)
    first_hooks = {}
    for m in range(KT // 2):
        first_hooks[2 * m] = [lambda m=m: wait(T, split_k[m])] + ([lambda m=m: modulate_step(m + 2)] if m + 2 < KT // 2 else [])
    stA = (AH, AL)
    u_sb = merged[:, 0, :].rearrange("p (a n) -> p a n", a=NT)
    wp = merged[:, 1, :].rearrange("p (a n) -> p a n", a=8)
    pool_w = a_load(wp, t["w_pool"][0].rearrange("g (a q) e -> q (g a) e", q=P), pool_in)
    ADA0 = 2 * D
    late = []

    def in_chunk(n, b, col, hooks=None):
        hooks = dict(hooks or {4: list(late)})
        late.clear()
        c = chunk(b, w_in, col, stA, ada=ADA0 + AC * n, hooks=hooks)
        d = ada_piece()
        late.append(lambda: ada_rows(d, AC * n, 2 + n % 2))
        return c

    for _ in range(AHEAD):
        split_part()
    c = in_chunk(0, 0, 0, first_hooks)
    wait(A, c)
    read_pair(0, A.copy(u_sb[:, :, 0:CH], pair[0]))
    wait(V, bias_in)
    p0.close()
    heads = scope()
    kT = sb("kT", [P, SBH, SEQ], c=heads)
    vv = sb("values", [P, NT, POOL_W], c=heads)
    YAH = sb("y_a_high", [P, 8, SEQ], F32R, c=heads)
    YAL = sb("y_a_low", [P, 8, SEQ], F32R, c=heads)
    pools = scope()
    qn = sb("qn", [P, NT, CH], c=pools)
    B0 = sb("band0", [P, 4, SEQ], c=pools)
    B1 = sb("band1", [P, 4, SEQ], c=pools)
    rc = sb("inverse_count", [P, SEQ], c=pools)
    pos = sb("positions", [P, SEQ], c=pools)
    pT = qn[:, :, :].rearrange("p a (h c) -> p (a h) c", c=SEQ)
    gg = sig(G.iota(rc[:, :].bitcast(I32), pattern=[[1, SEQ]], base=1, channel_multiplier=0), sG)
    wait(V, gg)
    pos_done = sig(V.tensor_copy(pos[:, :], rc[:, :].bitcast(I32)), sV)
    bands = {}

    def band(n):
        w = WINDOWS[n]
        take(V, "rc")
        wait(V, pos_done)
        v = sig(V.tensor_scalar(rc[:, :], pos[:, :], float(w), None, ALU.min), sV)
        wait(V, v)
        v = sig(V.reciprocal(rc[:, :], rc[:, :]), sV)
        wait(G, v)
        for to, first in ((B0, 0), (B1, P)):
            g = used("rc", sig(G.affine_select(out=to[:, n, :], in_=rc[:, :], compare_op=ALU.is_ge, fill=0.0, base=-first,
                                               pattern=[[1, SEQ]], channel_multiplier=-1), sG))
            wait(G, g)
            bands[n] = sig(G.affine_select(out=to[:, n, :], in_=to[:, n, :], compare_op=ALU.is_ge, fill=0.0, base=w - 1 + first,
                                           pattern=[[-1, SEQ]], channel_multiplier=1), sG)

    def minus_token(n):
        wait(V, bands[n])
        for to, first in ((B0, 0), (B1, P)):
            o = to[:, n, first:first + P]
            bands["done"] = sig(V.tensor_tensor(o, o, ident[:, :], ALU.subtract), sV)

    def head_norm(b, c, dst, i, norm):
        wait(A, c)
        take(A, "qn")
        a = sig(A.activation(qn[:, :, :], pair[b], ACT.Square), sA)
        wait(V, a)
        take(V, "ss")
        v = sig(V.tensor_reduce(ss[:, 0:8], qn[:, :, :].rearrange("p a (h d) -> p (a h) d", d=P), AX, ALU.add), sV)
        r = rsqrt(8, P, 1e-6, v)
        wait(V, r)
        q = read_pair(b, V.tensor_tensor(qn[:, :, :].rearrange("p a (h d) -> p (a h) d", d=P),
                                         pair[b].rearrange("p a (h d) -> p (a h) d", d=P),
                                         rs[:, 0:8].unsqueeze(2).broadcast_to([P, 8, P]), ALU.mult))
        used("rs", q)

        def finish():
            for half in range(2):
                m = used("qn", transposes(half, qn, 2 * half * P, [q]))
                wait(A, m)
                used(f"bank{half}", sig(A.activation(dst[:, ds(4 * i + 2 * half, 2), :], bank(half).rearrange(
                    "p (a c) -> p a c", c=SEQ), ACT.Copy, scale=cols2[:, at[norm]:at[norm] + 1]), sA))
        return finish

    for i in range(POOL_W // CH):
        if i > 0:
            c = in_chunk(4 * i, 0, CH * i)
            wait(A, c)
            read_pair(0, A.copy(u_sb[:, :, CH * i:CH * (i + 1)], pair[0]))
        hooks = {4: list(late)}
        if i == 0:
            for n in range(4):
                hooks.setdefault(3 * n + 1, []).append(lambda n=n: band(n))
                hooks.setdefault(3 * n + 4, []).append(lambda n=n: minus_token(n))
        c = in_chunk(4 * i + 1, 1, 3 * POOL_W + CH * i, hooks)
        wait(A, c)
        read_pair(1, A.copy(vv[:, :, CH * i:CH * (i + 1)], pair[1]))
        c = in_chunk(4 * i + 2, 0, POOL_W + CH * i)
        late.append(head_norm(0, c, qT, i, "q_norm"))
        c = in_chunk(4 * i + 3, 1, 2 * POOL_W + CH * i)
        late.append(head_norm(1, c, kT, i, "k_norm"))

    wait(T, bands["done"])

    def pooled_means(g4):
        b, h = 2 + g4 % 2, g4 % 2
        take(T, f"bank{b}")
        for half in range(2):
            o, ct = bank(b)[:, half * SEQ:(half + 1) * SEQ], 2 * g4 + half
            T.matmul(o, u_sb[:, 0, ct * P:(ct + 1) * P], B0[:, g4, :], start=True, stop=False)
            mm = T.matmul(o, u_sb[:, 1, ct * P:(ct + 1) * P], B1[:, g4, :], start=False, stop=True)
        m = sig(mm, sT)

        def keep():
            take(V, f"pT{h}")
            wait(V, m)
            return used(f"bank{b}", sig(V.tensor_copy(pT[:, 2 * h:2 * h + 2, :], bank(b).rearrange("p (a c) -> p a c", c=SEQ)), sV))
        return keep

    keep = pooled_means(2)
    for fn in late:
        fn()
    late.clear()
    last["pT0"], last["pT1"] = list(last["qn"]), list(last["qn"])
    pooled = {2: keep()}
    wait(T, pool_w)
    order = (2, 3, 0, 1)
    for g4 in order:
        if g4 != order[-1]:
            nxt = order[order.index(g4) + 1]
            pooled[nxt] = pooled_means(nxt)()
        b = g4 % 2
        take(T, f"bank{b}")
        wait(T, pooled[g4])
        for et in range(2):
            for ci in range(2):
                mm = T.matmul(bank(b)[:, et * SEQ:(et + 1) * SEQ], wp[:, 2 * g4 + ci, et * P:(et + 1) * P],
                              pT[:, 2 * (g4 % 2) + ci, :], start=(ci == 0), stop=(ci == 1))
        m = used(f"pT{g4 % 2}", sig(mm, sT))
        wait(A, m)
        ps, c0 = bank(b).rearrange("p (a c) -> p a c", c=SEQ), at["pool_scale"] + 2 * g4
        for j in range(2):
            h = sig(A.activation(YAH[:, 2 * g4 + j, :], ps[:, j, :], ACT.Copy, scale=cols2[:, c0 + j:c0 + j + 1]), sA)
        wait(V, h)
        for j in range(2):
            l = sig(V.scalar_tensor_tensor(out=YAL[:, 2 * g4 + j, :], in0=ps[:, j, :], scalar=cols2[:, c0 + j:c0 + j + 1],
                                           in1=YAH[:, 2 * g4 + j, :].bitcast(F32), op0=ALU.mult, op1=ALU.subtract), sV)
        used(f"bank{b}", l)
    wait(T, l)
    all_settled()
    pools.close()

    sbuf = scope()
    kS = sb("k_pair", [P, 2, SEQ], c=sbuf)
    vS = sb("v_pair", [P, NT, SEQ], c=sbuf)
    causal = sb("causal_t", [P, 2, SEQ], c=sbuf)
    later = sb("later", [P, P], c=sbuf)
    zl = sb("z_log", [P, 2, SEQ], c=sbuf)
    lb = sb("log_beta", [P, 2, 2, SEQ], c=sbuf)
    lm = sb("log_rest", [P, 2, 2, SEQ], c=sbuf)
    for j in range(2):
        G.memset(causal[:, j, :], 1.0)
    g = sig(G.memset(later[:, :], 1.0), sG)
    wait(G, g)
    for j in range(2):
        G.affine_select(out=causal[:, j, :], in_=causal[:, j, :], compare_op=ALU.is_gt, fill=0.0, base=-j * P,
                        pattern=[[1, SEQ]], channel_multiplier=-1)
    g = sig(G.affine_select(out=later[:, :], in_=later[:, :], compare_op=ALU.is_gt, fill=0.0, base=0,
                            pattern=[[-1, P]], channel_multiplier=1), sG)
    wait(V, g)
    wait(T, g)
    SCALE = float(P) ** -0.5

    def gate(b, c, dst):
        wait(A, c)
        a = read_pair(b, A.activation(dst, pair[b], ACT.Tanh, scale=0.5))
        wait(V, a)
        return sig(V.tensor_scalar(dst, dst, 0.5, 0.5, ALU.mult, ALU.add), sV)

    def heads_in(h0):
        take(V, "kS")
        a = sig(V.tensor_copy(kS[:, :, :], kT[:, ds(h0, 2), :]), sV)
        last["kS"] = [a]
        take(V, "vS")
        b = sig(V.tensor_copy(vS[:, :, :], vv[:, :, ds(P * h0, SEQ)]), sV)
        last["vS"] = [b]
        return b

    def sb_scores(hh, h0, ready):
        take(T, f"bank{hh}")
        wait(T, ready)
        for st in range(2):
            mm = T.matmul(bank(hh)[:, st * SEQ:(st + 1) * SEQ], kS[:, hh, st * P:(st + 1) * P],
                          qT[:, ds(h0 + hh, 1), :].rearrange("p a c -> p (a c)"), start=True, stop=True)
        m = used("kS", sig(mm, sT))
        ps = bank(hh).rearrange("p (a c) -> p a c", c=SEQ)
        take(A, "zl")
        wait(A, m)
        read = a = sig(A.activation(zl[:, :, :], ps, ACT.Abs, scale=SCALE), sA)
        wait(A, a)
        a = sig(A.activation(zl[:, :, :], zl[:, :, :], ACT.Exp, scale=-1.0), sA)
        wait(A, a)
        a = sig(A.activation(zl[:, :, :], zl[:, :, :], ACT.Ln, bias=1.0), sA)
        take(V, f"lb{hh}")
        wait(V, read)
        v = sig(V.tensor_scalar(lb[:, hh, :, :], ps, SCALE, 0.0, ALU.mult, ALU.min), sV)
        wait(V, v, a)
        v = used("zl", sig(V.tensor_tensor(lb[:, hh, :, :], lb[:, hh, :, :], zl[:, :, :], ALU.subtract), sV))
        take(V, f"lm{hh}")
        wait(V, v)
        w = used(f"bank{hh}", sig(V.scalar_tensor_tensor(out=lm[:, hh, :, :], in0=ps, scalar=-SCALE, in1=lb[:, hh, :, :],
                                                         op0=ALU.mult, op1=ALU.add), sV))
        wait(V, w)
        w = sig(V.tensor_tensor(lm[:, hh, :, :], lm[:, hh, :, :], causal[:, :, :], ALU.mult), sV)
        last[f"lm{hh}"] = [w]
        return v, w

    def sb_weights(hh, tok):
        take(T, "bank2")
        wait(T, tok[1])
        T.matmul(bank(2)[:, 0:SEQ], later[:, :], lm[:, hh, 0, :], start=True, stop=False)
        T.matmul(bank(2)[:, 0:SEQ], ones[:, :], lm[:, hh, 1, :], start=False, stop=True)
        m = used(f"lm{hh}", sig(T.matmul(bank(2)[:, SEQ:2 * SEQ], later[:, :], lm[:, hh, 1, :], start=True, stop=True), sT))
        wait(V, m)
        v = used("bank2", sig(V.tensor_tensor(lb[:, hh, :, :], bank(2).rearrange("p (a c) -> p a c", c=SEQ),
                                              lb[:, hh, :, :], ALU.add), sV))
        wait(V, v)
        v = sig(V.tensor_tensor(lb[:, hh, :, :], lb[:, hh, :, :], causal[:, :, :], ALU.mult), sV)
        wait(A, v)
        a = sig(A.activation(lb[:, hh, :, :], lb[:, hh, :, :], ACT.Exp), sA)
        wait(V, a)
        return sig(V.tensor_tensor(lb[:, hh, :, :], lb[:, hh, :, :], causal[:, :, :], ALU.mult), sV)

    def sb_out(hh, h0, ready):
        take(T, f"bank{hh}")
        wait(T, ready)
        for st in range(2):
            mm = T.matmul(bank(hh)[:, 0:SEQ], vS[:, st, hh * P:(hh + 1) * P], lb[:, hh, st, :],
                          start=(st == 0), stop=(st == 1))
        m = used(f"lb{hh}", used("vS", sig(mm, sT)))
        wait(A, m)
        used(f"bank{hh}", sig(A.copy(qT[:, ds(h0 + hh, 1), :].rearrange("p a c -> p (a c)"), bank(hh)[:, 0:SEQ]), sA))

    w_up = t["w_a_up"][0]
    with loop(2) as i:
        for n2 in range(2):
            col = 2 * CH * i + CH * n2
            h0 = 4 * i + 2 * n2
            st = {}
            hin = heads_in(h0)
            hooks = {2: [lambda: st.update(s0=sb_scores(0, h0, hin))],
                     5: [lambda: st.update(s1=sb_scores(1, h0, hin))],
                     9: [lambda: st.update(w0=sb_weights(0, st["s0"]))],
                     13: [lambda: st.update(w1=sb_weights(1, st["s1"]))]}
            c = chunk(0, w_in, 4 * POOL_W + col, stA, ada=ADA0 + D + 2 * AC * i + AC * n2, hooks=hooks)
            m_ = merged[:, :, ds(col, CH)]
            s = gate(0, c, m_)
            d1 = ada_piece()
            c = chunk(1, w_up, col, (YAH, YAL), nk=8,
                      hooks={2: [lambda: sb_out(0, h0, st["w0"])], 6: [lambda: sb_out(1, h0, st["w1"])]})
            wait(V, c, s)
            read_pair(1, V.tensor_tensor(m_, pair[1], m_, ALU.mult))
            ada_columns(d1, mod2[:, :, :].rearrange("p a b -> p (a b)")[:, ds(4 * i + 2 * n2, 2)], 3)
    sbuf.close()
    heads.close()

    up = scope()
    BH = sb("act_b_high", [P, KT, SEQ], F32R, c=up)
    BL = sb("act_b_low", [P, KT, SEQ], F32R, c=up)
    upb = scope()
    YBH = sb("y_b_high", [P, 8, SEQ], F32R, c=upb)
    YBL = sb("y_b_low", [P, 8, SEQ], F32R, c=upb)
    sg = qT[:, 0:4, :].rearrange("p (a h) c -> p a (h c)", a=NT)
    wait(A, *last["*"])
    wait(V, *last["*"])
    a = sig(A.copy(YBH[:, :, :], qT[:, :, :]), sA)
    wait(V, a)
    l = sig(V.tensor_tensor(YBL[:, :, :], qT[:, :, :], YBH[:, :, :].bitcast(F32), ALU.subtract), sV)
    wait(T, l)
    all_settled()
    w_up = t["w_b_up"][0]
    mod2_cols = mod2[:, :, :].rearrange("p a b -> p (a b)")
    for n in range(D // CH):
        pc = 4 + 2 * n
        c = chunk(0, w_in, 4 * POOL_W + D + CH * n, stA, ada=ADA0 + D + AC * pc, hooks={4: list(late)})
        late.clear()
        take(A, "sg")
        s = gate(0, c, sg[:, :, :])
        d1 = ada_piece()
        c = chunk(1, w_up, CH * n, (YBH, YBL), ada=ADA0 + D + AC * pc + AC, nk=8, hooks={
            4: [lambda: ada_columns(d1, mod2_cols[:, 2 * pc:2 * pc + 2], 2)]})
        wait(V, c, s)
        v = read_pair(1, V.tensor_tensor(sg[:, :, :], pair[1], sg[:, :, :], ALU.mult))
        wait(V, v)
        v = sig(V.tensor_tensor(sg[:, :, :], sg[:, :, :], merged[:, :, CH * n:CH * (n + 1)], ALU.add), sV)
        late.append(lambda v=v, n=n: turn(sg, "sg", [v], (BH, BL), 4 * n))
        late.append(lambda d=ada_piece(), pc=pc: ada_columns(d, mod2_cols[:, 2 * pc + 2:2 * pc + 4], 3))
    for fn in late:
        fn()
    late.clear()
    all_settled()
    upb.close()
    wait(T, *last["*"])

    def squares(n, ready, junk, name):
        take(A, name)
        wait(A, ready)
        for tt in range(NT):
            a = sig(A.activation(junk, x[:, tt, ds(CH * n, CH)], ACT.Square,
                                 accum_out=ssq[:, tt, ds(n, 1)]), sA)
            wait(A, a)
        return used("ssq", a)

    def sum_squares(ready, eps):
        take(V, "ss")
        wait(V, ready)
        v = used("ssq", sig(V.tensor_reduce(ss[:, 0:NT], ssq[:, :, :], AX, ALU.add), sV))
        return rsqrt(NT, D, eps, v)

    wo = scope()
    ot = sb("o_chunk", [P, NT, CH], c=wo)
    junk = sb("junk", [P, CH], c=wo)

    def add_gated(b, c, col, buf):
        take(V, "ot")
        wait(V, c)
        v = read_pair(b, V.tensor_tensor(buf[:, :, :], pair[b],
                                         gate_b[:, ds(col, CH)].unsqueeze(1).broadcast_to([P, NT, CH]), ALU.mult))
        wait(V, v)
        xs = x[:, :, ds(col, CH)]
        return used("gate_b", used("ot", sig(V.tensor_tensor(xs, xs, buf[:, :, :], ALU.add), sV)))

    with loop(2) as i:
        c = chunk(0, t["w_o"][0], 2 * CH * i, (BH, BL), ada=ADA0 + D + AC * (12 + 2 * i))
        d1 = ada_piece()
        v0 = add_gated(0, c, 2 * CH * i, ot)
        c = chunk(1, t["w_o"][0], 2 * CH * i + CH, (BH, BL), ada=ADA0 + D + AC * (13 + 2 * i), hooks={
            2: [lambda: squares(2 * i, v0, junk[:, :], "junk")],
            4: [lambda: ada_columns(d1, mod2[:, :, :].rearrange("p a b -> p (a b)")[:, ds(24 + 4 * i, 2)], 2)]})
        d2 = ada_piece()
        squares(2 * i + 1, add_gated(1, c, 2 * CH * i + CH, ot), junk[:, :], "junk")
        ada_columns(d2, mod2[:, :, :].rearrange("p a b -> p (a b)")[:, ds(26 + 4 * i, 2)], 3)
    wo.close()

    def norm_hooks(buf, eps, put, squared):
        wait(A, sum_squares(squared, eps))
        ready, split = {}, {}

        def scale(cc):
            take(A, f"xn{cc % 2}")
            for tt in range(NT):
                ready[cc] = used("rs", sig(A.activation(buf[:, cc % 2, tt, :], x[:, tt, cc * CH:(cc + 1) * CH], ACT.Copy,
                                                        scale=rs[:, tt:tt + 1]), sA))

        def step(m):
            cc, b = m // 2, m % 4
            t_ = used(f"xn{cc % 2}", transposes(b, buf[:, cc % 2, :, :], 2 * (m % 2) * P, [ready[cc]]))
            split[m] = put(2 * m, bank(b).rearrange("p (a c) -> p a c", c=SEQ), t_, b)

        scale(0)
        scale(1)
        step(0)
        step(1)
        hooks = {}
        for m in range(KT // 2):
            fns = [lambda m=m: wait(T, split[m])]
            if m + 2 < KT // 2:
                fns.append(lambda m=m: step(m + 2))
                if m % 2 == 0 and m // 2 + 2 < D // CH:
                    fns.append(lambda m=m: scale(m // 2 + 2))
            hooks[2 * m] = fns
        return hooks

    def put_weighted(col0):
        def put(k, ps, m, b):
            wait(A, m)
            for j in range(2):
                h = sig(A.activation(AH[:, k + j, :], ps[:, j, :], ACT.Copy, scale=cols2[:, col0 + k + j:col0 + k + j + 1]), sA)
            wait(V, h)
            for j in range(2):
                l = sig(V.scalar_tensor_tensor(out=AL[:, k + j, :], in0=ps[:, j, :], scalar=cols2[:, col0 + k + j:col0 + k + j + 1],
                                               in1=AH[:, k + j, :].bitcast(F32), op0=ALU.mult, op1=ALU.subtract), sV)
            return used(f"bank{b}", l)
        return put

    bias_in = (gate_in, gate_in.n + 16)
    wait(A, *last["*"])
    a_load(gate_b[:, :], t["b_ada"][0:1, 5 * D:6 * D].partition_broadcast(P), gate_in)
    ff = scope()
    buf = sb("ff_buf", [P, 2, NT, CH], c=ff)
    tmp = sb("ff_tmp", [P, 2, SEQ], c=ff)
    wait(V, *last["*"])
    v = sig(V.tensor_tensor(mod2[:, :, :].rearrange("p a b -> p (a b)"), mod2[:, :, :].rearrange("p a b -> p (a b)"),
                            cols1[:, 32 + 3 * KT:32 + 5 * KT], ALU.add), sV)
    wait(V, v)
    v = sig(V.scalar_tensor_tensor(out=mod2[:, 1, :], in0=mod2[:, 1, :], scalar=1.0,
                                   in1=cols2[:, at["norm2"]:at["norm2"] + KT], op0=ALU.add, op1=ALU.mult), sV)
    wait(A, v)

    def put_modulated(k, ps, m, b):
        wait(A, m)
        return modulate(ps, k, mod2, (AH, AL), tmp, b)

    acc = merged

    def mlp_group(i, first, final):
        row = D * i
        todo, piece, turned = [], [], []
        for n in range(4):
            b = n % 2
            c = chunk(b, t["w_ff1"][0], row + CH * n, stA, hooks=first if first and n == 0 else {4: todo, 12: piece},
                      ada={0: 5 * D + 2 * AC * i, 2: 5 * D + 2 * AC * i + AC}.get(n))
            piece = []
            take(A, f"xn{b}")
            wait(A, c)
            a = read_pair(b, A.activation(buf[:, b, :, :], pair[b], ACT.Relu))
            wait(A, a)
            f = sig(A.activation(buf[:, b, :, :], buf[:, b, :, :], ACT.Square), sA)
            todo = [lambda f=f, b=b, n=n: turned.append(turn(buf[:, b, :, :], f"xn{b}", [f], (BH, BL), 4 * n))]
            if n == 0:
                if first:
                    wait(V, bias_in)
                piece = [lambda d=ada_piece(): ada_rows(d, 2 * AC * i, 2)]
            if n == 2:
                piece = [lambda d=ada_piece(): ada_rows(d, 2 * AC * i + AC, 3)]
        for n in range(4):
            b = n % 2
            c = chunk(b, t["w_ff2"][0], CH * n, (BH, BL), row=row, hooks={
                0: [lambda: wait(T, turned[2])], 8: todo, 12: [lambda: wait(T, turned[3])]} if n == 0 else {})
            wait(V, c)
            cols = slice(CH * n, CH * (n + 1))
            xs = acc[:, :, cols]
            if first:
                read_pair(b, V.tensor_copy(xs, pair[b]))
                continue
            v = read_pair(b, V.tensor_tensor(xs, xs, pair[b], ALU.add))
            if final:
                wait(V, v)
                v = sig(V.tensor_tensor(xs, xs, gate_b[:, cols].unsqueeze(1).broadcast_to([P, NT, CH]), ALU.mult), sV)
                wait(V, v)
                v = sig(V.tensor_tensor(x[:, :, cols], x[:, :, cols], xs, ALU.add), sV)
                squared = squares(n, v, buf[:, 0, 0, :], "xn0")
        return squared if final else None

    mlp_group(0, norm_hooks(buf, 1e-6, put_modulated, now(sA)), False)
    with loop(D_FF // D - 2) as i:
        mlp_group(i + 1, None, False)
    squared = mlp_group(D_FF // D - 1, None, True)
    all_settled()
    ff.close()
    up.close()
    attn.close()

    blk = scope()
    zs = sb("zs", [P, NT, CH], c=blk)
    oo = sb("oo", [P, NT, CH], c=blk)
    qr = sb("qr", [P, NT, CH], c=blk)
    qG = sb("qG", [P, GH // 2, SEQ], c=blk)
    rt = sb("rope_tmp", [P, NT, GH, 16], c=blk)
    cc_ = sb("cos_cos", [P, NT, 16], c=blk)
    sn_ = sb("sin_sin", [P, NT, 16], c=blk)
    nsk = sb("minus_sinks", [P, GROUPS * GH], c=blk)
    nskg = sb("minus_sinks_group", [P, GH], c=blk)
    sc = sb("scores", [P, 4, 3 * P], c=blk)
    spare = ada_w[:, :, :, :].rearrange("p r a n -> p (r a n)")
    pt = spare[:, 0:12 * P].rearrange("p (s n) -> p s n", s=4)
    cpt = spare[:, 12 * P:14 * P].rearrange("p (a n) -> p a n", a=NT)
    mx = sb("row_max", [P, 2, GH, 2], c=blk)
    nm = sb("minus_max", [P, 2, GH, 2], c=blk)
    sm = sb("row_sum", [P, 2, GH, 2], c=blk)
    rd = sb("row_rec", [P, GH, 2], c=blk)
    kG = sb("keys_group", [P, SEQ], c=blk)
    kG2 = sb("keys_group_2", [P, SEQ], c=blk)
    kGc = sb("keys_group_cmp", [P, NC], c=blk)
    maskA = sb("mask_window", [P, 3 * P], c=blk)
    maskB = sb("mask_causal", [P, 3 * P], c=blk)

    sig(G.memset(maskA[:, :], 0.0), sG)
    g = sig(G.memset(maskB[:, :], 0.0), sG)
    wait(G, g)
    for mk, lo in ((maskA, True), (maskB, False)):
        for part in (0, 2):
            g = sig(G.affine_select(out=mk[:, part * P:(part + 1) * P], in_=mk[:, part * P:(part + 1) * P],
                                    compare_op=ALU.is_ge, fill=NEG, base=0, pattern=[[-1, P]], channel_multiplier=1), sG)
    g = sig(G.affine_select(out=maskA[:, P:2 * P], in_=maskA[:, P:2 * P], compare_op=ALU.is_gt, fill=NEG, base=0,
                            pattern=[[1, P]], channel_multiplier=-1), sG)

    posi = sb("pos_i", [P, NT], I32, c=blk)
    posf = sb("pos_f", [P, NT], c=blk)
    freq = sb("freq", [P, 8], c=blk)
    an = sb("angle", [P, NT, 8], c=blk)
    kk_ = sb("turns", [P, NT, 8], c=blk)
    ab = sb("abs_angle", [P, NT, 8], c=blk)
    wait(A, *last["*"])
    a_load(nsk[:, :], t["a_sinks_2"][0:1, :].partition_broadcast(P), kv_in)
    pos_in = a_load(posi[:, :], t["positions_2"].rearrange("a (b q) -> q (a b)", q=P), kv_in,
                    allow_slow_non_contiguous=True)
    inv_freq = np.float32(500000.0) ** (-np.arange(0, 16, 2, dtype=np.float32) / np.float32(16))
    for j in range(8):
        g = sig(G.memset(freq[:, j:j + 1], float(inv_freq[j])), sG)
    freq_done = g

    def rope_tables():
        wait(V, freq_done, pos_in)
        v = sig(V.tensor_copy(posf[:, :], posi[:, :]), sV)
        sig(V.tensor_scalar(nsk[:, :], nsk[:, :], -1.0, None, ALU.mult), sV)
        wait(V, v)
        for tt in range(NT):
            v = sig(V.tensor_scalar(an[:, tt, :], freq[:, :], posf[:, tt:tt + 1], None, ALU.mult), sV)
        wait(V, v)
        MAGIC = 1.5 * 2.0 ** 23
        v = sig(V.tensor_scalar(kk_[:, :, :], an[:, :, :], float(1 / (2 * np.pi)), MAGIC, ALU.mult, ALU.add), sV)
        wait(V, v)
        v = sig(V.tensor_scalar(kk_[:, :, :], kk_[:, :, :], -MAGIC, None, ALU.add), sV)
        wait(V, v)
        rest = 2 * np.pi
        for bits in (8, 11, None):
            part = float(np.float32(rest)) if bits is None else float(np.floor(rest * 2.0 ** (bits - 3)) / 2.0 ** (bits - 3)) \
                if bits == 8 else float(np.floor(rest * 2.0 ** 19) / 2.0 ** 19)
            rest -= part
            v = sig(V.scalar_tensor_tensor(out=an[:, :, :], in0=kk_[:, :, :], scalar=-part, in1=an[:, :, :],
                                           op0=ALU.mult, op1=ALU.add), sV)
            wait(V, v)
        v = sig(V.tensor_scalar(an[:, :, :], an[:, :, :], float(np.float32(3.1415925)), -float(np.float32(3.1415925)),
                                ALU.min, ALU.max), sV)
        wait(A, v)
        sig(A.activation(sn_[:, :, 8:16], an[:, :, :], ACT.Sin), sA)
        a = sig(A.activation(ab[:, :, :], an[:, :, :], ACT.Abs), sA)
        wait(V, a)
        v = sig(V.tensor_scalar(sn_[:, :, 0:8], sn_[:, :, 8:16], -1.0, None, ALU.mult), sV)
        v = sig(V.tensor_scalar(ab[:, :, :], ab[:, :, :], -1.0, float(np.pi / 2), ALU.mult, ALU.add), sV)
        wait(A, v)
        sig(A.activation(cc_[:, :, 0:8], ab[:, :, :], ACT.Sin), sA)
        a = sig(A.activation(cc_[:, :, 8:16], ab[:, :, :], ACT.Sin), sA)
        wait(V, a)

    def rotate(src, nh, ready):
        take(V, "rt")
        wait(V, *ready)
        c3 = cc_[:, :, :].unsqueeze(2).broadcast_to([P, NT, nh, 16])
        tmp_ = rt[:, :, 0:nh, :]
        sig(V.tensor_tensor(tmp_[:, :, :, 0:8], src[:, :, :, 8:16], sn_[:, :, 0:8].unsqueeze(2).broadcast_to([P, NT, nh, 8]), ALU.mult), sV)
        v = sig(V.tensor_tensor(tmp_[:, :, :, 8:16], src[:, :, :, 0:8], sn_[:, :, 8:16].unsqueeze(2).broadcast_to([P, NT, nh, 8]), ALU.mult), sV)
        wait(V, v)
        v = sig(V.tensor_tensor(src[:, :, :, 0:16], src[:, :, :, 0:16], c3, ALU.mult), sV)
        wait(V, v)
        v = sig(V.tensor_tensor(src[:, :, :, 0:16], src[:, :, :, 0:16], tmp_, ALU.add), sV)
        last["rt"] = [v]
        return v

    def kv_chunk(b, w, col, k2, vdst, dup, rot, shift=False, hooks=None):
        c = chunk(b, w, col, stA, hooks=hooks)
        take(A, "dup")
        wait(A, c)
        psk = pair[b][:, :, 0:SEQ].rearrange("p a (g d) -> p a g d", d=HD)
        if vdst is not None:
            sig(A.copy(vdst, pair[b][:, :, SEQ:CH]), sA)
        a = read_pair(b, A.copy(dup[:, :, :, 0, :], psk))
        v = rotate(dup[:, :, :, 0, :], GROUPS, [a]) if rot else a
        wait(V, v)
        v = sig(V.tensor_copy(dup[:, :, :, 1, :], dup[:, :, :, 0, :]), sV)
        flat = dup.rearrange("p a g e d -> p a (g e d)")

        def finish():
            for half in range(2):
                m = used("dup", transposes(half, flat, 2 * half * P, [v]))
                wait(A, m)
                ps = bank(half).rearrange("p (a c) -> p a c", c=SEQ)
                kd = k2[:, 2 * half:2 * half + 2, :]
                if shift:
                    sig(A.copy(kd[0:HD, :, :], ps[0:HD, :, :]), sA)
                    used(f"bank{half}", sig(A.copy(kd[HD:P, :, 0:SEQ - 1], ps[HD:P, :, 1:SEQ]), sA))
                else:
                    used(f"bank{half}", sig(A.copy(kd, ps), sA))
            return now(sA)
        return finish

    def q_chunk(b, w, col, hooks=None):
        c = chunk(b, w, col, stA, hooks=hooks)
        take(A, "qr")
        wait(A, c)
        a = read_pair(b, A.copy(qr[:, :, :], pair[b]))
        last["qr"] = [rotate(qr[:, :, :].rearrange("p a (h d) -> p a h d", d=HD), GH, [a])]

    def q_turn():
        take(A, "qG")
        for half in range(2):
            m = transposes(half, qr, 2 * half * P, last.get("qr", last["*"]) if half == 0 else [])
            wait(A, m)
            a = used(f"bank{half}", sig(A.copy(qG[:, 2 * half:2 * half + 2, :], bank(half).rearrange("p (a c) -> p a c", c=SEQ)), sA))
        last["qr"], last["qG"] = [m], [a]
        return a

    def head_scores(j, br, kG, mask, ready, sinks):
        o = (j % 2) * HD
        s = j % 4
        take(T, "bank1")
        wait(T, *ready)
        for tt in range(NT):
            c0, n = (0, P) if tt == 0 else (P, SEQ)
            mm = T.matmul(bank(1)[:, c0:c0 + n], qG[o:o + HD, j // 2, tt * P:(tt + 1) * P],
                          kG[o:o + HD, 0:n], start=True, stop=True)
        m = used("qG", sig(mm, sT))
        take(V, f"sc{s}")
        wait(V, m)
        v = used("bank1", sig(V.tensor_tensor(sc[:, s, :], bank(1)[:, 0:3 * P], mask[:, :], ALU.add), sV))
        take(V, f"mx{br}{j}")
        wait(V, v)
        sig(V.tensor_reduce(mx[:, br, j, 0:1], sc[:, s, 0:P], AX, ALU.max), sV)
        v = sig(V.tensor_reduce(mx[:, br, j, 1:2], sc[:, s, P:3 * P], AX, ALU.max), sV)
        wait(V, v)
        if sinks:
            v = sig(V.tensor_scalar(nm[:, br, j, :], mx[:, br, j, :], -HD ** -0.5, nskg[:, j:j + 1], ALU.mult, ALU.min), sV)
        else:
            v = sig(V.tensor_scalar(nm[:, br, j, :], mx[:, br, j, :], -HD ** -0.5, None, ALU.mult), sV)
        wait(A, v)
        for tt in range(NT):
            c0, n = (0, P) if tt == 0 else (P, SEQ)
            a = sig(A.activation(sc[:, s, c0:c0 + n], sc[:, s, c0:c0 + n], ACT.Exp, scale=HD ** -0.5,
                                 bias=nm[:, br, j, tt:tt + 1], accum_out=sm[:, br, j, tt:tt + 1]), sA)
        used(f"mx{br}{j}", a)
        return a

    def head_turn(j, ready):
        s = j % 4
        take(T, "bank0")
        wait(T, ready)
        for q in range(3):
            tr = T.transpose(bank(0)[:, q * P:(q + 1) * P], sc[:, s, q * P:(q + 1) * P], ident[:, :])
        m = used(f"sc{s}", sig(tr, sT))
        take(A, f"pt{s}")
        wait(A, m)
        return used("bank0", sig(A.copy(pt[:, s, :], bank(0)[:, 0:3 * P]), sA))

    def head_values(j, vals, gi, ready):
        s = j % 4
        if j == 0:
            take(T, "bank2")
            take(T, "bank3")
        wait(T, ready)
        oc = slice(j * HD, (j + 1) * HD)
        T.matmul(bank(2)[:, oc], pt[:, s, 0:P], vals[:, 0, ds(gi * HD, HD)], start=True, stop=True)
        T.matmul(bank(3)[:, oc], pt[:, s, P:2 * P], vals[:, 0, ds(gi * HD, HD)], start=True, stop=False)
        return used(f"pt{s}", sig(T.matmul(bank(3)[:, oc], pt[:, s, 2 * P:3 * P], vals[:, 1, ds(gi * HD, HD)],
                                           start=False, stop=True), sT))

    def group_copy(dst, src, gi):
        take(A, dst.name)
        a = sig(A.copy(dst[:, :], src[:, ds(gi, 1), :].rearrange("p a c -> p (a c)")), sA)
        last[dst.name] = [a]
        return a

    def attention(first, gap, br, kG, vals, gi, mask, ready, sinks, end):
        tok, ev = {}, []
        for j in range(GH):
            k = first + int(gap * j)
            ev.append((k + 4, lambda j=j: tok.update({("v", j): head_values(j, vals, gi, tok["t", j])})))
            ev.append((k + 2, lambda j=j: tok.update({("t", j): head_turn(j, tok["s", j])})))
            ev.append((k, lambda j=j: tok.update({("s", j): head_scores(j, br, kG, mask, ready(), sinks)})))
        ev.append((k + 5, lambda: end(tok["s", GH - 1], tok["v", GH - 1])))
        return ev

    def hooks_of(events, c):
        hooks = {}
        for k, fn in sorted(events, key=lambda e: e[0]):
            if k // KT == c:
                hooks.setdefault(k % KT, []).append(fn)
        return hooks

    def group_chunks(gi, w, zcol, qcol, events, dst, w_out, final=False):
        st = {}
        events = events + [(28, lambda: st.update(o=gate_outputs(st["z"]))),
                           (29, lambda: turn(oo, "oo", [st["o"]], dst, 4 * gi))]
        if qcol is None:
            events = [(min(k, 27), fn) if k >= 28 else (k, fn) for k, fn in events] + [(28, lambda: wait(T, now(sV)))]
        c = chunk(1, w, zcol, stA, hooks=hooks_of(events, 0))
        st["z"] = silu_z(1, c)
        if qcol is not None:
            q_chunk(0, w, qcol, hooks=hooks_of(events, 1))
        else:
            return out_product(w_out, dst, hooks_of(events, 1), final)

    def silu_z(b, c):
        take(A, "zs")
        wait(A, c)
        a = sig(A.activation(zs[:, :, :], pair[b], ACT.Tanh, scale=0.5), sA)
        wait(V, a)
        return read_pair(b, V.scalar_tensor_tensor(out=zs[:, :, :], in0=zs[:, :, :], scalar=1.0, in1=pair[b],
                                                   op0=ALU.add, op1=ALU.mult))

    def heads_view(ap):
        return ap.rearrange("p (h d) -> p h d", d=HD)

    def gate_outputs(z):
        wait(V, z, *last["oo"])
        return used("zs", sig(V.tensor_tensor(oo[:, :, :], oo[:, :, :], zs[:, :, :], ALU.mult), sV))

    def out_product(w, stat, hooks, final):
        for n in range(D // CH):
            b = n % 2
            c = chunk(b, w, CH * n, stat, hooks=hooks if n == 0 else None, final=final and n == D // CH - 1)
            wait(V, c)
            xs = x[:, :, CH * n:CH * (n + 1)]
            v = read_pair(b, V.tensor_tensor(xs, xs, pair[b], ALU.add))
            s_ = squares(n, v, zs[:, 0, :], "zs")
        return s_

    mixa = scope()
    k2 = sb("a_keys", [P, GROUPS, SEQ], c=mixa)
    va = gate_b[:, 0:NT * SEQ].rearrange("p (a n) -> p a n", a=NT)
    dup = sb("a_dup", [P, NT, GROUPS, 2, HD], c=mixa)[:, :, :, :, :]
    norms = scope()
    buf = sb("a_buf", [P, 2, NT, CH], c=norms)
    w_a = t["a_w_in_2"][0]
    hooks = norm_hooks(buf, 1e-5, put_weighted(at["norm_2"]), squared)
    hooks[KT - 1] = [rope_tables]
    kv_chunk(0, w_a, D, k2, va[:, :, :], dup, True, hooks=hooks)()
    norms.close()
    scope()
    BH = sb("act_c_high", [P, KT, SEQ], F32R, c=mixa)
    BL = sb("act_c_low", [P, KT, SEQ], F32R, c=mixa)
    all_settled()
    q_chunk(0, w_a, 0)

    def group_a(gi, qcol):
        nq = sig(V.tensor_copy(nskg[:, :], nsk[:, ds(GH * gi, GH)]), sV)
        wait(V, nq)
        st = {}

        def end(s, v_):
            wait(V, s)
            take(V, "rd")
            v = sig(V.tensor_tensor(rd[:, :, :], nm[:, 0, :, :], nskg[:, :].unsqueeze(2).broadcast_to([P, GH, 2]), ALU.subtract), sV)
            wait(A, v)
            a = sig(A.activation(rd[:, :, :], rd[:, :, :], ACT.Exp), sA)
            wait(V, a)
            v = sig(V.tensor_tensor(rd[:, :, :], rd[:, :, :], sm[:, 0, :, :], ALU.add), sV)
            wait(V, v)
            v = sig(V.reciprocal(rd[:, :, :], rd[:, :, :]), sV)
            wait(V, v)
            v = sig(V.tensor_scalar(rd[:, :, :], rd[:, :, :], 0.5, None, ALU.mult), sV)
            wait(V, v, v_)
            take(V, "oo")
            for tt in range(NT):
                v = used(f"bank{2 + tt}", sig(V.tensor_tensor(
                    heads_view(oo[:, tt, :]), heads_view(bank(2 + tt)),
                    rd[:, :, tt].unsqueeze(2).broadcast_to([P, GH, HD]), ALU.mult), sV))
            last["oo"] = [v]

        events = [(1, lambda: group_copy(kG, k2, gi)), (1, lambda: st.update(q=q_turn()))] + attention(
            3, 2, 0, kG, va, gi, maskA, lambda: [st["q"]], True, end)
        return group_chunks(gi, w_a, D + CH + CH * gi, qcol, events, (BH, BL), t["a_w_out_2"][0])

    with loop(GROUPS - 1) as i:
        group_a(i, CH * i + CH)
    squared = group_a(GROUPS - 1, None)
    all_settled()
    mixa.close()

    mixb = scope()
    ks2 = sb("b_keys_sel", [P, GROUPS, SEQ], c=mixb)
    kw2 = sb("b_keys_win", [P, GROUPS, SEQ], c=mixb)
    vs = sb("b_values_sel", [P, NT, SEQ], c=mixb)
    vw = sb("b_values_win", [P, NT, SEQ], c=mixb)
    gts = sb("b_gates", [P, NT, 96], c=mixb)
    kcT = sb("b_keys_cmp", [P, GROUPS, NC], c=mixb)
    vbd = gate_b[:, :].rearrange("p (g n) -> p g n", g=GROUPS)
    maskC = sb("mask_cmp", [P, NT, NC], c=mixb)
    cmp = scope()
    buf = sb("b_buf", [P, 2, NT, CH], c=cmp)
    dup = oo[:, :, :].rearrange("p a (g e d) -> p a g e d", e=2, d=HD)
    kc2 = zs[:, :, :].rearrange("p a n -> p (a n)").rearrange("p (g n) -> p g n", g=GROUPS)
    vc2 = qr[:, :, :].rearrange("p a n -> p (a n)").rearrange("p (g n) -> p g n", g=GROUPS)
    w1 = sb("w1_sb", [P, KT, SEQ], c=cmp)
    w_b = t["b_w_in_2"][0]
    wait(A, *last["*"])
    w1k = a_load(w1[:, :, :], t["b_cmp_k_w1_2"][0].rearrange("(k q) n -> q k n", q=P), kv_in)
    c = chunk(0, w_b, D, stA, hooks=norm_hooks(buf, 1e-5, put_weighted(at["norm_2"] + KT), squared))
    for src0, k2_ in ((0, kc2), (SEQ, vc2)):
        take(A, "dup")
        wait(A, c)
        psk = pair[0][:, :, src0:src0 + SEQ].rearrange("p a (g d) -> p a g d", d=HD)
        sig(A.copy(dup[:, :, :, 0, :], psk), sA)
        a = sig(A.copy(dup[:, :, :, 1, :], psk), sA)
        flat = dup.rearrange("p a g e d -> p a (g e d)")
        for half in range(2):
            m = used("dup", transposes(half, flat, 2 * half * P, [a]))
            wait(A, m)
            ps = bank(half).rearrange("p (a c) -> p a c", c=SEQ)
            kd = k2_[:, 2 * half:2 * half + 2, :]
            sig(A.copy(kd[0:HD, :, :], ps[0:HD, :, :]), sA)
            kc_done = used(f"bank{half}", sig(A.copy(kd[HD:P, :, 0:SEQ - 1], ps[HD:P, :, 1:SEQ]), sA))
    last["pair0"] = [kc_done]
    f1 = kv_chunk(1, w_b, D + CH, ks2, vs[:, :, :], dup, True)
    f1()
    f2 = kv_chunk(0, w_b, D + 2 * CH, kw2, vw[:, :, :], dup, True)
    load_unit(w_b[:, D + 3 * CH:D + 3 * CH + 96].rearrange("(k p) n -> p k n", p=P), k=KT, n=96)
    take(T, "pair1")
    for k in range(KT):
        if k % (KT // HALF) == 0:
            split_part()
        ktile(1, k, KT, stA, k % (KT // HALF), (k + 1) % (KT // HALF) == 0, width=96)
    wait(A, now(unit_done))
    a = read_pair(1, A.activation(gts[:, :, :], pair[1][:, :, 0:96], ACT.Tanh, scale=0.5))
    wait(V, a)
    sig(V.tensor_scalar(gts[:, :, :], gts[:, :, :], 0.5, 0.5, ALU.mult, ALU.add), sV)
    f2()

    NK = GROUPS * NC
    bt = sb("blocksT", [P, KT, NK], c=cmp)
    ge = sb("hidden", [NK, SEQ], c=cmp)
    hidT = sb("hiddenT", [P, 2, NK], c=cmp)
    w2 = sb("w2_sb", [P, 2, 2, HD], c=cmp)
    vg = sb("v_cmp", [NC, GROUPS, HD], c=cmp)
    rep = sb("repeat", [NC, GH, NC], c=cmp)
    bdm = ada_acc[0:GH * NC, :, :].rearrange("p a n -> p (a n)").rearrange("p (h d) -> p h d", d=HD)
    g = sig(G.memset(rep[:, :, :], 0.0), sG)
    g = sig(G.memset(bdm[:, :, :], 1.0), sG)
    g = sig(G.memset(maskC[:, :, :], 0.0), sG)
    wait(G, g)
    sig(G.affine_select(out=rep[:, :, :], in_=rep[:, :, :], compare_op=ALU.not_equal, fill=1.0, base=0,
                        pattern=[[0, GH], [-1, NC]], channel_multiplier=1), sG)
    g = sig(G.affine_select(out=bdm[:, :, :], in_=bdm[:, :, :], compare_op=ALU.is_ge, fill=0.0, base=0,
                            pattern=[[-NC, GH], [0, HD]], channel_multiplier=1), sG)
    wait(G, g)
    sig(G.affine_select(out=bdm[:, :, :], in_=bdm[:, :, :], compare_op=ALU.is_ge, fill=0.0, base=NC - 1,
                        pattern=[[NC, GH], [0, HD]], channel_multiplier=-1), sG)
    bdone = sig(G.affine_select(out=maskC[:, :, :], in_=maskC[:, :, :], compare_op=ALU.is_ge, fill=NEG, base=-31,
                                pattern=[[P, NT], [-16, NC]], channel_multiplier=1), sG)
    wait(V, bdone)
    wait(T, bdone)
    for which, src, w_2, pos in ((0, kc2, "b_cmp_k_w2_2", "pos_k"), (1, vc2, "b_cmp_v_w2_2", "pos_v")):
        take(A, "w2")
        a_load(w2[:, :, 0, :], t[w_2][0].rearrange("(k q) n -> q k n", q=P), kv_in)
        w2_in = a_load(w2[:, :, 1, :], t[w_2][0].rearrange("(k q) n -> q k n", q=P), kv_in)
        take(V, "bt")
        wait(V, kc_done)
        for j in range(KT):
            blocks = src[:, :, 2 * j:2 * j + 16 * (NC - 1) + 1:16]
            v = sig(V.tensor_scalar(bt[:, j, :].rearrange("p (g n) -> p g n", n=NC), blocks,
                                    cols2[:, at[pos] + j:at[pos] + j + 1], None, ALU.add), sV)
        wait(T, v, w1k, w2_in)
        take(T, "bank0")
        for j in range(KT):
            mm = T.matmul(bank(0)[0:NK, 0:SEQ], bt[:, j, :], w1[:, j, :], start=(j == 0), stop=(j == KT - 1))
        m = used("bt", sig(mm, sT))
        if which == 0:
            wait(A, m)
            w1k = a_load(w1[:, :, :], t["b_cmp_v_w1_2"][0].rearrange("(k q) n -> q k n", q=P), kv_in)
        ps, gf = bank(0)[0:NK, 0:SEQ], ge[:, :]
        take(A, "ge")
        wait(A, m)
        a = sig(A.activation(gf, ps, ACT.Square), sA)
        wait(V, a)
        v = sig(V.tensor_scalar(gf, gf, 0.044715, 1.0, ALU.mult, ALU.add), sV)
        wait(V, v)
        v = sig(V.tensor_tensor(gf, gf, ps, ALU.mult), sV)
        wait(A, v)
        a = sig(A.activation(gf, gf, ACT.Tanh, scale=float(np.sqrt(2 / np.pi))), sA)
        wait(V, a)
        v = sig(V.tensor_scalar(gf, gf, 0.5, 0.5, ALU.mult, ALU.add), sV)
        wait(V, v)
        v = used("bank0", sig(V.tensor_tensor(gf, gf, ps, ALU.mult), sV))
        take(T, "bank1")
        wait(T, v)
        for k in range(2):
            tr = T.transpose(bank(1)[:, k * NK:(k + 1) * NK], ge[:, k * P:(k + 1) * P], ident[0:NK, 0:NK])
        m = used("ge", sig(tr, sT))
        take(V, "hidT")
        wait(V, m)
        v = used("bank1", sig(V.tensor_copy(hidT[:, :, :], bank(1)[:, 0:2 * NK].rearrange("p (a n) -> p a n", a=2)), sV))
        wait(T, v)
        take(T, "bank1")
        if which == 0:
            for k in range(2):
                mm = T.matmul(bank(1)[:, 0:NK], w2[:, k, :, :].rearrange("p a b -> p (a b)"), hidT[:, k, :],
                              start=(k == 0), stop=(k == 1))
            m = used("w2", used("hidT", sig(mm, sT)))
            wait(V, m)
            used("bank1", sig(V.tensor_copy(kcT[:, :, :], bank(1)[:, 0:NK].rearrange("p (g n) -> p g n", n=NC)), sV))
        else:
            for gq in range(GROUPS):
                for k in range(2):
                    mm = T.matmul(bank(1)[0:NC, gq * HD:(gq + 1) * HD], hidT[:, k, gq * NC:(gq + 1) * NC], w2[:, k, 0, :],
                                  start=(k == 0), stop=(k == 1))
            m = sig(mm, sT)
            wait(V, m)
            v = used("bank1", sig(V.tensor_copy(vg[:, :, :], bank(1)[0:NC, 0:GROUPS * HD].rearrange("p (g n) -> p g n", n=HD)), sV))
            wait(T, v)
            for gq in range(GROUPS):
                b = 2 + gq % 2
                take(T, f"bank{b}")
                m = sig(T.matmul(bank(b)[0:GH * NC, :], rep[:, :, :].rearrange("p a b -> p (a b)"),
                                 vg[:, gq, :].unsqueeze(1).broadcast_to([NC, GH, HD]), start=True, stop=True), sT)
                wait(V, m)
                v = used(f"bank{b}", sig(V.tensor_tensor(vbd[0:GH * NC, gq, :].rearrange("p (h d) -> p h d", d=HD),
                                                         heads_view(bank(b)[0:GH * NC, :]), bdm[:, :, :], ALU.mult), sV))
            wait(T, v)
    all_settled()
    cmp.close()
    BH = sb("act_d_high", [P, KT, SEQ], F32R, c=mixb)
    BL = sb("act_d_low", [P, KT, SEQ], F32R, c=mixb)
    cs = spare[:, 14 * P:14 * P + NT * GH * NC].rearrange("p (a h n) -> p a h n", a=NT, h=GH)
    cm = sb("cmp_max", [P, NT, GH], c=mixb)
    cg = sb("cmp_gate", [P, NT, GH], c=mixb)
    gr = sb("gate_rec", [P, NT, GH], c=mixb)
    ob = ada_acc[:, :, :].rearrange("p a n -> p (a n)")
    R = HD ** -0.5
    HB = GH * NC

    q_chunk(0, w_b, 0)

    def group_b(gi, qcol):
        st = {}

        def turned():
            for to, src in ((kG, ks2), (kG2, kw2), (kGc, kcT)):
                group_copy(to, src, gi)
            st["q"] = q_turn()

        def cmp_scores():
            take(T, "bank0")
            take(T, "bank1")
            wait(T, st["q"])
            for j in range(GH):
                o = (j % 2) * HD
                for tt in range(NT):
                    c0 = (tt * GH // 2 + j // 2) * NC
                    mm = T.matmul(bank(j % 2)[:, c0:c0 + NC], qG[o:o + HD, j // 2, tt * P:(tt + 1) * P],
                                  kGc[o:o + HD, :], start=True, stop=True)
            m = used("qG", sig(mm, sT))
            take(V, "cs")
            wait(V, m)
            for e in range(2):
                for tt in range(NT):
                    v = sig(V.tensor_tensor(cs[:, tt, e:GH:2, :],
                                            bank(e)[:, tt * HB // 2:(tt + 1) * HB // 2].rearrange("p (h n) -> p h n", n=NC),
                                            maskC[:, tt, :].unsqueeze(1).broadcast_to([P, GH // 2, NC]), ALU.add), sV)
                used(f"bank{e}", v)
            wait(V, v)
            csf = cs[:, :, :, :].rearrange("p a h n -> p (a h) n")
            cmf = cm[:, :, :].rearrange("p a h -> p (a h)")
            v = sig(V.tensor_reduce(cmf, csf, AX, ALU.max), sV)
            wait(V, v)
            v = sig(V.tensor_scalar(cmf, cmf, 0.1 * NEG, None, ALU.max), sV)
            wait(V, v)
            v = sig(V.tensor_tensor(csf, csf, cmf.unsqueeze(2).broadcast_to([P, NT * GH, NC]), ALU.subtract), sV)
            wait(A, v)
            a = sig(A.activation(cs[:, :, :, :], cs[:, :, :, :], ACT.Exp, scale=R), sA)
            wait(V, a)
            v = sig(V.tensor_reduce(cmf, csf, AX, ALU.add), sV)
            wait(V, v)
            v = sig(V.tensor_scalar(cmf, cmf, 1e-30, 2.0, ALU.max, ALU.mult), sV)
            wait(V, v)
            v = sig(V.reciprocal(cmf, cmf), sV)
            wait(V, v)
            v = sig(V.tensor_tensor(cg[:, :, :], cm[:, :, :], gts[:, :, ds(GH * gi, GH)], ALU.mult), sV)
            wait(V, v)
            st["cs"] = sig(V.tensor_tensor(csf, csf, cg[:, :, :].rearrange("p a h -> p (a h)").unsqueeze(2)
                                           .broadcast_to([P, NT * GH, NC]), ALU.mult), sV)

        def cmp_turn():
            take(T, "bank0")
            wait(T, st["cs"])
            for tt in range(NT):
                tr = T.transpose(bank(0)[0:HB, tt * P:(tt + 1) * P], cs[:, tt, :, :].rearrange("p h n -> p (h n)"), ident[:, :])
            m = used("cs", sig(tr, sT))
            take(A, "cpt")
            wait(A, m)
            st["cpt"] = used("bank0", sig(A.copy(cpt[0:HB, :, :], bank(0)[0:HB, 0:SEQ].rearrange("p (a c) -> p a c", c=P)), sA))

        def cmp_values():
            take(T, "bank2")
            take(T, "bank3")
            wait(T, st["cpt"])
            for tt in range(NT):
                mm = T.matmul(bank(2 + tt), cpt[0:HB, tt, :], vbd[0:HB, ds(gi, 1), :].rearrange("p a c -> p (a c)"), start=True, stop=True)
            m = used("cpt", sig(mm, sT))
            take(V, "oo")
            wait(V, m)
            for tt in range(NT):
                v = used(f"bank{2 + tt}", sig(V.tensor_copy(oo[:, tt, :], bank(2 + tt)), sV))
            last["oo"] = [v]

        def add_branch(n):
            def end(s, v_):
                wait(V, s)
                take(V, "rd")
                v = sig(V.tensor_scalar(rd[:, :, :], sm[:, n - 1, :, :], 2.0, None, ALU.mult), sV)
                wait(V, v)
                v = sig(V.reciprocal(rd[:, :, :], rd[:, :, :]), sV)
                wait(V, v)
                v = sig(V.tensor_tensor(gr[:, :, :], rd[:, :, :].rearrange("p h a -> p a h"),
                                        gts[:, :, ds(32 * n + GH * gi, GH)], ALU.mult), sV)
                wait(V, v, v_)
                for tt in range(NT):
                    v = used(f"bank{2 + tt}", sig(V.tensor_tensor(
                        heads_view(ob), heads_view(bank(2 + tt)), gr[:, tt, :].unsqueeze(2).broadcast_to([P, GH, HD]), ALU.mult), sV))
                    wait(V, v, *last["oo"])
                    v = sig(V.tensor_tensor(oo[:, tt, :], oo[:, tt, :], ob, ALU.add), sV)
                    wait(V, v)
                last["oo"] = [v]
            return end

        ready = lambda: [st["q"]]
        events = [(1, turned), (2, cmp_scores), (5, cmp_turn), (7, cmp_values)]
        events += attention(4, 1.25, 0, kG, vs, gi, maskB, ready, False, add_branch(1))
        events += attention(14, 1.25, 1, kG2, vw, gi, maskB, ready, False, add_branch(2))
        return group_chunks(gi, w_b, D + 3 * CH + 96 + CH * gi, qcol, events, (BH, BL), t["b_w_out_2"][0], final=True)

    with loop(GROUPS - 1) as i:
        group_b(i, CH * i + CH)
    squared = group_b(GROUPS - 1, None)
    all_settled()
    wf = gate_b
    wait(A, *last["*"])
    wf_in = a_load(wf[:, :], t["final_norm_w_2"].rearrange("(a n) -> a n", a=1).partition_broadcast(P), end_in)
    mixb.close()
    fin = scope()
    y = sb("y", [P, NT, D], c=fin)
    r = sum_squares(squared, 1e-5)
    wait(V, r, wf_in)
    for tt in range(NT):
        for h in range(2):
            cols = slice(h * D // 2, (h + 1) * D // 2)
            v = sig(V.scalar_tensor_tensor(out=y[:, tt, cols], in0=x[:, tt, cols], scalar=rs[:, tt:tt + 1],
                                           in1=wf[:, cols], op0=ALU.mult, op1=ALU.mult), sV)
            wait(S, v)
            o = sig(S.dma_start(t["out"][0, tt * P:(tt + 1) * P, cols], y[:, tt, cols]), out_in, 16)
    wait(S, o)
    fin.close()
    blk.close()


_INS = ["x", "c", "w_ada", "b_ada", "norm1_w", "w_in", "q_norm_w", "k_norm_w", "w_pool", "pool_scale", "w_a_up",
        "w_b_up", "w_o", "norm2_w", "w_ff1", "w_ff2", "positions_2", "norm_w_2", "final_norm_w_2", "a_w_in_2",
        "a_sinks_2", "a_w_out_2", "b_w_in_2", "b_cmp_k_pos_2", "b_cmp_k_w1_2", "b_cmp_k_w2_2", "b_cmp_v_pos_2",
        "b_cmp_v_w1_2", "b_cmp_v_w2_2", "b_w_out_2"]


def kernel(**inputs):
    import concourse.bacc as bacc
    from concourse.bass_utils import run_bass_kernel_spmd

    arrays = {f"in_{n}": np.ascontiguousarray(inputs[n]) for n in _INS}

    def program(per_loop):
        nc = bacc.Bacc("TRN2", target_bir_lowering=False, num_devices=1)
        t = {n: nc.dram_tensor(f"in_{n}", arrays[f"in_{n}"].shape, mybir.dt.from_np(arrays[f"in_{n}"].dtype),
                               kind="ExternalInput").ap() for n in _INS}
        t["out"] = nc.dram_tensor("out", (1, SEQ, D), F32, kind="ExternalOutput").ap()
        build(nc, t, per_loop)
        return nc

    per_loop = {}
    program(per_loop)
    nc = program(per_loop)
    r = run_bass_kernel_spmd(nc, [arrays], core_ids=[0])
    return r.results[0]["out"]
```
